# Optimizing a Trainium2 kernel written in Bass

```python
import math
import jax, jax.numpy as jnp
from jax import lax
import numpy as np

D_MODEL = 1024
BATCH = 1
SEQ = 1024
DEPTH = 1
DEC_BATCH = 8
DEC_SEQ = 1
PAST_LEN = 8192
PAGE_SIZE = 128

D_MIX = D_MODEL
N_HEADS_A = 8
HEAD_DIM_A = 64
N_KV_A = 2
N_HEADS_IDX = 8
HEAD_DIM_IDX = 64
TOPK_MAX = 256
Q_BLOCK = 128
N_HEADS_R = 8
DK_R = 64
DV_R = (D_MIX - N_HEADS_A * HEAD_DIM_A) // N_HEADS_R
HGRN_CHUNK = 64
D_FF = 2816
LN_EPS = 1e-5
RMS_EPS = 1e-6
DN_ALPHA = (2 * DEPTH) ** 0.25
DN_BETA = (8 * DEPTH) ** -0.25

A_Q = N_HEADS_A * HEAD_DIM_A
A_KV = N_KV_A * HEAD_DIM_A
I_Q = N_HEADS_IDX * HEAD_DIM_IDX
I_K = HEAD_DIM_IDX
I_W = N_HEADS_IDX
R_QF = N_HEADS_R * DK_R
R_V = N_HEADS_R * DV_R
SPLIT_SIZES = (A_Q, A_KV, A_KV, I_Q, I_K, I_W, R_QF, R_QF, R_V, R_V)
SPLIT_POINTS = tuple(int(s) for s in np.cumsum(SPLIT_SIZES)[:-1])
D_IN = int(sum(SPLIT_SIZES))

kernel_name = "hymba_dsa_hgrn2_macaron_deepnorm_step"

F32 = jnp.float32

def layer_norm(x, g, b):
    x32 = x.astype(F32)
    mu = jnp.mean(x32, -1, keepdims=True)
    xc = x32 - mu
    var = jnp.mean(xc * xc, -1, keepdims=True)
    return (xc * lax.rsqrt(var + LN_EPS) * g.astype(F32) + b.astype(F32)).astype(x.dtype)

def swiglu(x, wg, wu, wd):
    return (jax.nn.silu(x @ wg) * (x @ wu)) @ wd

def ffn_sublayer(x, wg, wu, wd, g, b):
    return layer_norm(DN_ALPHA * x + 0.5 * swiglu(x, wg, wu, wd), g, b)

def split_projection(h, w_in):
    return jnp.split(h @ w_in, SPLIT_POINTS, axis=-1)

def gather_rows(rows, idx):
    return jax.vmap(lambda a, i: a[i])(rows, idx)

def indexer_scores(qi, wi, kidx, valid):
    logits = jnp.einsum('bqhd,bld->bqhl', qi.astype(F32), kidx.astype(F32)) * (HEAD_DIM_IDX ** -0.5)
    score = jnp.einsum('bqh,bqhl->bql', wi.astype(F32) * (N_HEADS_IDX ** -0.5), jax.nn.relu(logits))
    return jnp.where(valid, score, -jnp.inf)

def sparse_attend(q, k_sel, v_sel, valid):
    B, Q, H, DH = q.shape
    G = k_sel.shape[3]
    qg = q.astype(F32).reshape(B, Q, G, H // G, DH)
    s = jnp.einsum('bqgrd,bqkgd->bqgrk', qg, k_sel.astype(F32)) * (DH ** -0.5)
    s = jnp.where(valid[:, :, None, None, :], s, -jnp.inf)
    p = jax.nn.softmax(s, axis=-1)
    o = jnp.einsum('bqgrk,bqkgd->bqgrd', p, v_sel.astype(F32))
    return o.reshape(B, Q, H * DH).astype(q.dtype)

def hgrn_lower_bound(lb_param, layer):
    return jnp.cumsum(jax.nn.softmax(lb_param.astype(F32), axis=0), axis=0)[layer]

def hgrn2_recurrence(q, k, v, logf, s0, chunk):
    B, T, H, DK = q.shape
    DV = v.shape[-1]
    n = T // chunk

    def to_chunks(a):
        return a.reshape(B, n, chunk, H, a.shape[-1]).transpose(1, 0, 3, 2, 4)

    tri = jnp.tril(jnp.ones((chunk, chunk), bool))[None, None, :, :, None]

    def step(S, inp):
        qc, kc, vc, gc = inp
        b = jnp.cumsum(gc, axis=2)
        diff = b[:, :, :, None, :] - b[:, :, None, :, :]
        decay = jnp.exp(jnp.where(tri, diff, -jnp.inf))
        A = jnp.einsum('bhtd,bhsd,bhtsd->bhts', qc, kc, decay)
        o = jnp.einsum('bhts,bhse->bhte', A, vc) + jnp.einsum('bhtd,bhde->bhte', qc * jnp.exp(b), S)
        b_last = b[:, :, -1:, :]
        S = jnp.exp(b_last[:, :, 0, :])[..., None] * S + jnp.einsum('bhsd,bhse->bhde', kc * jnp.exp(b_last - b), vc)
        return S, o

    S, o = lax.scan(step, s0, (to_chunks(q), to_chunks(k), to_chunks(v), to_chunks(logf)))
    o = o.transpose(1, 0, 3, 2, 4).reshape(B, T, H, DV)
    return o, S

def hgrn2_branch(rq, rf, ri, rg, lb, norm_g, s0, chunk):
    B, T, _ = rq.shape
    f = lb + (1.0 - lb) * jax.nn.sigmoid(rf.astype(F32))
    logf = jnp.log(f)
    kk = 1.0 - f
    shp = (B, T, N_HEADS_R, DK_R)
    o, s_new = hgrn2_recurrence(rq.astype(F32).reshape(shp), kk.reshape(shp),
                                ri.astype(F32).reshape(B, T, N_HEADS_R, DV_R),
                                logf.reshape(shp), s0.astype(F32), chunk)
    o = o * lax.rsqrt(jnp.mean(o * o, -1, keepdims=True) + RMS_EPS)
    o = o.reshape(B, T, R_V) * norm_g.astype(F32) * jax.nn.silu(rg.astype(F32))
    return o.astype(rq.dtype), s_new.astype(rq.dtype)

def mixer_prompt(h, w_in, w_out, lb, norm_g):
    B, S, _ = h.shape
    q, k, v, qi, ki, wi, rq, rf, ri, rg = split_projection(h, w_in)
    q = q.reshape(B, S, N_HEADS_A, HEAD_DIM_A)
    k = k.reshape(B, S, N_KV_A, HEAD_DIM_A)
    v = v.reshape(B, S, N_KV_A, HEAD_DIM_A)
    qi = qi.reshape(B, S, N_HEADS_IDX, HEAD_DIM_IDX)
    n_sel = min(TOPK_MAX, S // 4)
    qbs = min(Q_BLOCK, S)
    nb = S // qbs
    key_pos = jnp.arange(S)

    def blocks(a):
        return a.reshape((B, nb, qbs) + a.shape[2:]).swapaxes(0, 1)

    def attend_block(args):
        q_b, qi_b, w_b, start = args
        pos = start + jnp.arange(qbs)
        valid = key_pos[None, :] <= pos[:, None]
        score = indexer_scores(qi_b, w_b, ki, valid[None])
        _, idx = lax.top_k(score, n_sel)
        flat = idx.reshape(B, qbs * n_sel)
        k_sel = gather_rows(k, flat).reshape(B, qbs, n_sel, N_KV_A, HEAD_DIM_A)
        v_sel = gather_rows(v, flat).reshape(B, qbs, n_sel, N_KV_A, HEAD_DIM_A)
        return sparse_attend(q_b, k_sel, v_sel, idx <= pos[None, :, None])

    starts = jnp.arange(nb, dtype=jnp.int32) * qbs
    o_attn = lax.map(attend_block, (blocks(q), blocks(qi), blocks(wi), starts))
    o_attn = o_attn.swapaxes(0, 1).reshape(B, S, A_Q)
    s0 = jnp.zeros((B, N_HEADS_R, DK_R, DV_R), F32)
    o_r, s_new = hgrn2_branch(rq, rf, ri, rg, lb, norm_g, s0, min(HGRN_CHUNK, S))
    m = jnp.concatenate([o_attn, o_r], axis=-1) @ w_out
    return m, k, v, ki, s_new

def mixer_sample(h, cache_k, cache_v, cache_kidx, state, page_table, w_in, w_out, lb, norm_g):
    B, T, _ = h.shape
    q, k, v, qi, ki, wi, rq, rf, ri, rg = split_projection(h, w_in)
    q = q.reshape(B, T, N_HEADS_A, HEAD_DIM_A)
    k = k.reshape(B, T, N_KV_A, HEAD_DIM_A)
    v = v.reshape(B, T, N_KV_A, HEAD_DIM_A)
    qi = qi.reshape(B, T, N_HEADS_IDX, HEAD_DIM_IDX)
    n_pages = page_table.shape[1]
    past = n_pages * PAGE_SIZE
    L = past + T
    n_sel = min(TOPK_MAX, L // 4)
    ki_past = cache_kidx[page_table].reshape(B, past, HEAD_DIM_IDX).astype(ki.dtype)
    ki_all = jnp.concatenate([ki_past, ki], axis=1)
    pos = past + jnp.arange(T)
    valid = jnp.arange(L)[None, :] <= pos[:, None]
    score = indexer_scores(qi, wi, ki_all, valid[None])
    _, idx = lax.top_k(score, n_sel)
    in_past = (idx < past)[..., None, None]
    pidx = jnp.minimum(idx, past - 1)
    phys = page_table[jnp.arange(B)[:, None, None], pidx // PAGE_SIZE]
    off = pidx % PAGE_SIZE
    nidx = jnp.clip(idx - past, 0, T - 1).reshape(B, T * n_sel)
    k_new = gather_rows(k, nidx).reshape(B, T, n_sel, N_KV_A, HEAD_DIM_A)
    v_new = gather_rows(v, nidx).reshape(B, T, n_sel, N_KV_A, HEAD_DIM_A)
    k_sel = jnp.where(in_past, cache_k[phys, off].astype(k.dtype), k_new)
    v_sel = jnp.where(in_past, cache_v[phys, off].astype(v.dtype), v_new)
    o_attn = sparse_attend(q, k_sel, v_sel, idx <= pos[None, :, None])
    o_r, s_new = hgrn2_branch(rq, rf, ri, rg, lb, norm_g, state, T)
    m = jnp.concatenate([o_attn, o_r], axis=-1) @ w_out
    return m, k, v, ki, s_new

def setup_inputs(seed: int = 0) -> dict:
    key = jax.random.key(seed)
    ks = jax.random.split(key, 32)
    n_pages = PAST_LEN // PAGE_SIZE
    n_used = DEC_BATCH * n_pages
    n_phys = n_used + max(1, n_used // 4)

    def nrm(k, shape, scale=1.0):
        return jax.random.normal(k, shape, F32) * scale

    def gain(k, shape):
        return 1.0 + 0.02 * jax.random.normal(k, shape, F32)

    page_table = jax.random.permutation(ks[0], n_phys)[:n_used].reshape(DEC_BATCH, n_pages).astype(jnp.int32)
    return {
        "x_prompt": nrm(ks[1], (BATCH, SEQ, D_MODEL)),
        "x_sample": nrm(ks[2], (DEC_BATCH, DEC_SEQ, D_MODEL)),
        "cache_k": nrm(ks[3], (DEPTH, n_phys, PAGE_SIZE, N_KV_A, HEAD_DIM_A)),
        "cache_v": nrm(ks[4], (DEPTH, n_phys, PAGE_SIZE, N_KV_A, HEAD_DIM_A)),
        "cache_kidx": nrm(ks[5], (DEPTH, n_phys, PAGE_SIZE, HEAD_DIM_IDX)),
        "state_hgrn": nrm(ks[6], (DEPTH, DEC_BATCH, N_HEADS_R, DK_R, DV_R), 0.5),
        "page_table": page_table,
        "w_in": nrm(ks[7], (DEPTH, D_MODEL, D_IN), D_MODEL ** -0.5),
        "w_out": nrm(ks[8], (DEPTH, D_MIX, D_MODEL), DN_BETA * D_MIX ** -0.5),
        "hgrn_lb": nrm(ks[9], (DEPTH + 1, R_QF)),
        "hgrn_norm_g": gain(ks[10], (DEPTH, R_V)),
        "ffn1_wg": nrm(ks[11], (DEPTH, D_MODEL, D_FF), D_MODEL ** -0.5),
        "ffn1_wu": nrm(ks[12], (DEPTH, D_MODEL, D_FF), D_MODEL ** -0.5),
        "ffn1_wd": nrm(ks[13], (DEPTH, D_FF, D_MODEL), DN_BETA * D_FF ** -0.5),
        "ffn2_wg": nrm(ks[14], (DEPTH, D_MODEL, D_FF), D_MODEL ** -0.5),
        "ffn2_wu": nrm(ks[15], (DEPTH, D_MODEL, D_FF), D_MODEL ** -0.5),
        "ffn2_wd": nrm(ks[16], (DEPTH, D_FF, D_MODEL), DN_BETA * D_FF ** -0.5),
        "ln1_g": gain(ks[17], (DEPTH, D_MODEL)),
        "ln1_b": nrm(ks[18], (DEPTH, D_MODEL), 0.02),
        "ln2_g": gain(ks[19], (DEPTH, D_MODEL)),
        "ln2_b": nrm(ks[20], (DEPTH, D_MODEL), 0.02),
        "ln3_g": gain(ks[21], (DEPTH, D_MODEL)),
        "ln3_b": nrm(ks[22], (DEPTH, D_MODEL), 0.02),
    }

def reference(x_prompt, x_sample, cache_k, cache_v, cache_kidx, state_hgrn, page_table,
              w_in, w_out, hgrn_lb, hgrn_norm_g,
              ffn1_wg, ffn1_wu, ffn1_wd, ffn2_wg, ffn2_wu, ffn2_wd,
              ln1_g, ln1_b, ln2_g, ln2_b, ln3_g, ln3_b):
    yp, ys = x_prompt, x_sample
    kp_l, vp_l, kip_l, sp_l = [], [], [], []
    ks_l, vs_l, kis_l, ss_l = [], [], [], []
    for l in range(DEPTH):
        lb = hgrn_lower_bound(hgrn_lb, l)
        hp = ffn_sublayer(yp, ffn1_wg[l], ffn1_wu[l], ffn1_wd[l], ln1_g[l], ln1_b[l])
        hs = ffn_sublayer(ys, ffn1_wg[l], ffn1_wu[l], ffn1_wd[l], ln1_g[l], ln1_b[l])
        mp, kp, vp, kip, sp = mixer_prompt(hp, w_in[l], w_out[l], lb, hgrn_norm_g[l])
        ms, ksn, vsn, kisn, ssn = mixer_sample(hs, cache_k[l], cache_v[l], cache_kidx[l], state_hgrn[l],
                                            page_table, w_in[l], w_out[l], lb, hgrn_norm_g[l])
        hp = layer_norm(DN_ALPHA * hp + mp, ln2_g[l], ln2_b[l])
        hs = layer_norm(DN_ALPHA * hs + ms, ln2_g[l], ln2_b[l])
        yp = ffn_sublayer(hp, ffn2_wg[l], ffn2_wu[l], ffn2_wd[l], ln3_g[l], ln3_b[l])
        ys = ffn_sublayer(hs, ffn2_wg[l], ffn2_wu[l], ffn2_wd[l], ln3_g[l], ln3_b[l])
        kp_l.append(kp); vp_l.append(vp); kip_l.append(kip); sp_l.append(sp)
        ks_l.append(ksn); vs_l.append(vsn); kis_l.append(kisn); ss_l.append(ssn)
    k_prompt = jnp.stack(kp_l)
    v_prompt = jnp.stack(vp_l)
    kidx_prompt = jnp.stack(kip_l)
    state_prompt = jnp.stack(sp_l)
    k_sample = jnp.stack(ks_l)
    v_sample = jnp.stack(vs_l)
    kidx_sample = jnp.stack(kis_l)
    state_sample = jnp.stack(ss_l)
    return (yp, ys, k_prompt, v_prompt, kidx_prompt, state_prompt, k_sample, v_sample, kidx_sample, state_sample)


_drawn_inputs = setup_inputs


def setup_inputs(seed=0):
    import zlib

    import numpy as np

    out = dict(_drawn_inputs(seed))
    spreads = {}
    factors = {'hgrn_norm_g': 23.426,
     'ln2_g': 2.817,
     'ln2_b': 2.911,
     'ln3_g': 7.572,
     'ln3_b': 7.774,
     'cache_k': 3.427,
     'cache_v': 2.736,
     'cache_kidx': 2.822}
    for name, (base, spread) in spreads.items():
        noise = np.random.default_rng([zlib.crc32(name.encode()), seed]).standard_normal(out[name].shape)
        drawn = base * np.exp(spread * noise) if base else spread * noise
        out[name] = __import__('jax').numpy.asarray(drawn.astype(out[name].dtype))
    for name, factor in factors.items():
        out[name] = (out[name] * factor).astype(out[name].dtype)
    return out
```

```python
import math
from contextlib import ExitStack

import numpy as np

import concourse.bass as bass
from concourse import mybir


def build_decoder_step(nc, I, O):
    f32, u32, i32 = mybir.dt.float32, mybir.dt.uint32, mybir.dt.int32
    ALU, ACT, AX = mybir.AluOpType, mybir.ActivationFunctionType, mybir.AxisListType

    P = 128
    D = 1024
    DT = D // P
    SEQ, NB = 1024, 8
    TOK = SEQ + NB
    TG = 3
    TW = TOK // TG
    BLK = SEQ // P
    FF = 2816
    FT = FF // P
    SLAB = 256
    NSLAB = FF // SLAB
    H, HD, GRP = 8, 64, 2
    TOPK = 256
    PAGE, NPAGES, NPHYS = 128, 64, 640
    FIRST_TOPK = TOPK // P
    QB0, KB0, QI0, KI0, RQ0, RF0, RI0, RG0 = 0, 512, 768, 1280, 1352, 1864, 2376, 2888
    ALPHA = 2.0 ** 0.25
    LN_EPS, RMS_EPS = 1e-5, 1e-6
    NEG = -3.0e38
    MASKED = 1.0e30
    KSCALE = HD ** -0.5

    ctx = ExitStack()
    with ctx:
        def sb(name, shape, dt=f32):
            return ctx.enter_context(nc.sbuf_tensor(name, shape, dt))

        def sem(name):
            return ctx.enter_context(nc.semaphore(name))

        def dram(name, shape):
            return nc.dram_tensor(name, shape, f32, kind="Internal").ap()

        ACTS = sb("acts", [P, DT, TOK])
        BIG = sb("big", [P, FT * TOK])
        RING = sb("weight_ring", [P, 4, DT * SLAB])
        WD = sb("down_weights", [P, 2, FT * P])
        TMP = sb("tmp", [P, 4 * TOK])
        AUX = sb("aux", [P, 2048])
        PS = ctx.enter_context(nc.psum_tensor("ps", [P, 8, 512], f32))
        IDENT = sb("ident", [P, P])
        MEAN1 = sb("mean_ones", [P, P])
        HALF1 = sb("half_ones", [P, P])
        TRI = sb("tri", [P, P])
        ROW63 = sb("row63", [P, 2, NB])
        CAUSAL = sb("causal", [P, 2 * P])
        LEVELS = sb("level_masks", [P, 7, P], mybir.dt.uint8)
        PARAMS = sb("params", [P, 6, DT])
        LB = sb("lower_bound", [P, 4, 4])
        BITS = sb("bits", [P, 33], u32)
        IOTA = sb("iota_slots", [P, TOPK])
        SLOT = sb("slot", [P, 2])
        CAND = sb("candidate", [P, 10], u32)
        FOUND = sb("found", [P, 10], u32)
        REJ = sb("rejected", [P, 10], u32)
        CNT = sb("counts", [P, 10])
        SMALL = sb("small", [P, 240])
        PGI = sb("page_ids", [P, 4], i32)
        PGX = sb("page_rows", [P, 8, 4], u32)
        GIDX = sb("gather_rows", [P, 16], u32)

        HT = BIG[:, :].rearrange("p (f t) -> p f t", t=TOK)
        XIN = BIG[:, 0:9 * D].rearrange("p (b d) -> p b d", d=D)
        C4 = 4 * TOK
        QIT = BIG[:, 0:C4].rearrange("p (f t) -> p f t", t=TOK)
        QT = BIG[:, C4:2 * C4].rearrange("p (f t) -> p f t", t=TOK)
        RI = BIG[:, 2 * C4:2 * C4 + 4096].rearrange("p (b c) -> p b c", c=512)
        OTA, OTR = QIT, BIG[:, 2 * C4:3 * C4].rearrange("p (f t) -> p f t", t=TOK)
        RG = BIG[:, 3 * C4:3 * C4 + 9 * 512].rearrange("p (b c) -> p b c", c=512)
        o_k3 = 3 * C4 + 9 * 512
        K3 = BIG[:, o_k3:o_k3 + 3 * TOK].rearrange("p (g t) -> p g t", t=TOK)
        o_kv = o_k3 + 3 * TOK
        KV = BIG[:, o_kv:o_kv + 9 * 256].rearrange("p (b c) -> p b c", c=256)
        assert o_kv + 9 * 256 <= FT * TOK
        SQ = BIG[:, 3 * C4:3 * C4 + 2 * DT * TW].rearrange("p (u d t) -> p u d t", u=2, d=DT)
        SG = TMP[:, 0:TOK].rearrange("p (g t) -> p g t", t=TW)
        SUM = TMP[:, TOK:2 * TOK].rearrange("p (g t) -> p g t", t=TW)
        VAR = TMP[:, 2 * TOK:3 * TOK].rearrange("p (g t) -> p g t", t=TW)
        RSTD = TMP[:, 3 * TOK:4 * TOK].rearrange("p (g t) -> p g t", t=TW)
        XOUT = BIG[:, 0:2 * D].rearrange("p (u d) -> p u d", d=D)

        x_loaded, x_turned, x_ready = sem("x_loaded"), sem("x_turned"), sem("x_ready")
        consts, params_in, consts2 = sem("consts_built"), sem("params_loaded"), sem("consts2_built")
        ring_in = [sem(f"ring_loaded{s}") for s in range(4)]
        wd_in = [sem(f"down_loaded{s}") for s in range(2)]
        up_done = sem("up_done")
        silu_done = sem("silu_done")
        h_done = sem("hidden_done")
        y_done = sem("y_done")
        z_done = sem("z_done")
        ln_sum = sem("ln_sum")
        ln_mean = sem("ln_mean")
        ln_xc = sem("ln_centred")
        ln_sq = sem("ln_squared")
        ln_vs = sem("ln_sqsum")
        ln_var = sem("ln_var")
        ln_sd = sem("ln_sd")
        ln_n = sem("ln_normed")
        ln_done = sem("ln_done")
        y_turned, y_copied = sem("out_turned"), sem("out_copied")
        y_stored = [sem(f"out_stored{s}") for s in range(2)]
        dve_step, act_step, pool_step = sem("dve_step"), sem("act_step"), sem("pool_step")

        w_in = I["w_in"][0].rearrange("(k p) n -> p k n", p=P)
        w_out = I["w_out"][0].rearrange("(k p) n -> p k n", p=P)
        MIX = [[(w_in, QI0, 256)], [(w_in, QI0 + 256, 256)], [(w_in, KB0, 256)], [(w_in, KI0, 72)],
               [(w_in, QB0, 256)], [(w_in, QB0 + 256, 256)], [(w_in, RI0, 256)], [(w_in, RI0 + 256, 256)],
               [(w_in, RG0, 256)], [(w_in, RG0 + 256, 256)]]
        MIX += [[(w_in, RF0 + P * t, P), (w_in, RQ0 + P * t, P)] for t in range(4)]
        MIX += [[(w_out, SLAB * s, SLAB)] for s in range(4)]
        ITEM0 = [0, 2 * NSLAB + len(MIX)]
        MIX0 = 2 * NSLAB
        assert ITEM0[1] % 4 == 0
        reach, total = {}, [0, 0, 0, 0]
        for n in range(ITEM0[1] + 2 * NSLAB):
            parts = len(MIX[n - MIX0]) if MIX0 <= n < ITEM0[1] else 1
            total[n % 4] += 16 * parts
            reach[n] = total[n % 4]
        EPS = SMALL[:, 232:236]

        MIXER = True

        KX = QT_ = BIG[:, C4:C4 + 4096].rearrange("p (u c) -> p u c", c=1024)
        KD = BIG[:, 2 * C4 + 2304:2 * C4 + 3072].rearrange("p (u c) -> p u c", c=384)
        KXT = BIG[:, 2 * C4:2 * C4 + 2048].rearrange("p (u c) -> p u c", c=1024)
        DPROD = BIG[:, 2 * C4 + 2048:2 * C4 + 2304].rearrange("p (u c) -> p u c", c=P)
        RELU = BIG[:, 3 * C4:3 * C4 + 2048].rearrange("p (u c) -> p u c", c=1024)
        QITOK = BIG[0:NB, 3 * C4 + 2048:3 * C4 + 2560].rearrange("p (h d) -> p h d", d=HD)
        QIPROD = BIG[0:NB, 3 * C4 + 2560:3 * C4 + 3072].rearrange("p (h d) -> p h d", d=HD)
        SCORE_AT = {b: P * sum(range(FIRST_TOPK + 1, b + 1)) for b in range(FIRST_TOPK, BLK)}
        WDF = WD[:, :, :].rearrange("p s c -> p (s c)")

        def score(b):
            return WDF[:, SCORE_AT[b]:SCORE_AT[b] + P * (b + 1)]
        o_wd = P * sum(range(FIRST_TOPK + 1, BLK + 1))
        RIS = WDF[0:NB, o_wd:o_wd + 512]
        SDEC = WDF[:, o_wd + 512:o_wd + 512 + 516].rearrange("p (g k) -> p g k", k=PAGE + 1)
        SDECF = WDF[:, o_wd + 512:o_wd + 512 + 516]
        HD3 = WDF[:, o_wd + 1028:o_wd + 1124].rearrange("p (w t b) -> p w t b", w=3, t=4)
        QB = WDF[:, o_wd + 1124:o_wd + 1252].rearrange("p (r h b) -> p r h b", r=2, h=H)
        assert o_wd + 1252 <= 2 * FT * P
        KIW = AUX[:, 0:9 * 72].rearrange("p (b c) -> p b c", c=72)
        WIS = AUX[:, 648:648 + 72].rearrange("p (b h) -> p b h", h=H)
        JUNK = BIG[:, o_kv + 2304:o_kv + 2560].bitcast(mybir.dt.uint8)
        DCMP = K3[:, 2, 9 * HD:9 * HD + 258].bitcast(mybir.dt.bfloat16).rearrange("p (g k) -> p g k", k=PAGE + 1)
        DEQ, DRK = TMP[:, 1540:2056], TMP[:, 2056:2572]
        DGT = TMP[:, 1024:1540]
        RESET = TMP[:, 2572:3088]
        o_hot = 2 * TOK
        DONE_HOT = BIG[:, o_hot:o_hot + 1024].rearrange("p (g r) -> p g r", r=TOPK)
        DRANK = BIG[:, o_hot + 1024:o_hot + 1540].rearrange("p (g k) -> p g k", k=PAGE + 1)
        DJUNK = BIG[:, o_hot + 1540:o_hot + 1540 + P]
        EQ, PRE, GT = TMP[:, 1024:2048], TMP[:, 2048:3072], TMP[:, 3072:4096]
        HQ, HF, HK = (BIG[:, TOK * i:TOK * (i + 1)] for i in range(3))
        PF, SF = BIG[:, 3 * TOK:3 * TOK + SEQ], TMP[:, 0:1024]
        LV = TMP[:, 1024:3072].rearrange("p (u t) -> p u t", t=SEQ)
        KTOK = TMP[:, 3072:4096].rearrange("p (c x) -> p c x", x=P)
        AT = AUX[:, :].rearrange("p (u c t) -> p u c t", u=2, c=BLK)
        SC = K3[:, 2, 0:9 * HD].rearrange("p (c e) -> p c e", e=HD)
        OSQ = LV[:, 0, :]
        SM = TMP[:, 0:2048].rearrange("p (u c) -> p u c", c=1024)
        PT = TMP[:, 2048:4096].rearrange("p (u c) -> p u c", c=1024)
        OTOK = AUX[:, 0:1024].rearrange("p (u c) -> p u c", c=512)
        KS = BIG[:, 2 * C4:2 * C4 + 2048].rearrange("p (j c) -> p j c", c=P)
        VS = BIG[:, 2 * C4 + 2048:2 * C4 + 4096].rearrange("p (j c) -> p j c", c=P)
        KTD = TMP[:, 0:2056].rearrange("p (b c) -> p b c", c=TOPK + 1)
        SDD = TMP[0:H, 2056:4112].rearrange("p (b c) -> p b c", c=TOPK + 1)
        PTD = AUX[:, 0:P].rearrange("p (j h) -> p j h", h=H)
        PTN = AUX[0:1, P:P + 64].rearrange("p (b h) -> p b h", h=H)
        QD = AUX[:, 192:256].rearrange("p (h b) -> p h b", b=NB)
        OD = AUX[0:H, 1024:2048].rearrange("p (b c) -> p b c", c=P)
        VN = K3[0:1, 2, 0:1024].rearrange("p (b c) -> p b c", c=P)
        S0 = BIG[:, C4:C4 + 2048].rearrange("p (t b e) -> p t b e", t=4, b=NB)
        VB = BIG[:, C4 + 2048:C4 + 4096].rearrange("p (t b e) -> p t b e", t=4, b=NB)
        T1 = WDF[:, 0:2048].rearrange("p (t b e) -> p t b e", t=4, b=NB)
        T2 = WDF[:, 2048:4096].rearrange("p (t b e) -> p t b e", t=4, b=NB)
        OR2 = BIG[0:2, C4:C4 + 2048].rearrange("p (t b e) -> p t b e", t=4, b=NB)
        OD8 = BIG[0:NB, o_k3:o_k3 + 1024]
        OD8SQ = BIG[0:NB, o_k3 + 1024:o_k3 + 1536]
        NORMG = sb("norm_g", [P, 512])
        WDEC = SMALL[:, 0:32].rearrange("p (g h) -> p g h", h=H)
        DCNT, GTC, PCC = SMALL[:, 32:36], SMALL[:, 36:40], SMALL[:, 40:48]
        NEED, EXCL, INCL = SMALL[:, 48:52], SMALL[:, 52:56], SMALL[:, 56:60]
        KEY, PG = SMALL[:, 64:80], SMALL[:, 80:96]
        NMX, MX = SMALL[:, 96:98], SMALL[:, 98:100]
        SUMS = SMALL[:, 104:120].rearrange("p (u h) -> p u h", h=H)
        RSUM = SMALL[:, 120:128]
        SS, SR = SMALL[:, 128:144], SMALL[:, 144:160]
        CGP, NEEDP = SMALL[:, 160:166], SMALL[:, 166:172]
        DL, SN = SMALL[0:NB, 172:180], SMALL[0:NB, 180:181]
        NF, DMX, DSUM = SMALL[0:H, 184:192], SMALL[0:H, 192:200], SMALL[0:H, 200:208]
        NFW = SMALL[0:H, 208:216]
        DSS = SMALL[0:NB, 216:224]

        qi_s, q_s = dram("scratch_qi", [512, NB]), dram("scratch_q", [512, NB])
        w_s, sn_s = dram("scratch_w", [NB, H]), dram("scratch_new_score", [NB, 1])
        ri_s, o_s, or_s = dram("scratch_ri", [NB, 512]), dram("scratch_o", [NB, 512]), dram("scratch_or", [NB, 512])

        maps_built, levels_built, pages_in, pgx_ready = sem("maps_built"), sem("levels_built"), sem("pages_in"), sem("pgx_ready")
        lb_in, lb_diff, lb_sig, lb_ready = sem("lb_in"), sem("lb_diff"), sem("lb_sig"), sem("lb_ready")
        unit_done, unit_out = sem("unit_done"), sem("unit_out")
        kd_ready = sem("kd_ready")
        wis_ready, k_turned, k3_ready = sem("wis_ready"), sem("k_turned"), sem("k3_ready")
        qid_turned, sn_ready = sem("qid_turned"), sem("sn_ready")
        qi_out, qb_zero, qb_in, w_outd, w_in_dec, sn_out, sn_in = (sem(x) for x in (
            "qi_scratch", "qb_zeroed", "qb_in", "w_scratch", "wdec_in", "sn_scratch", "sn_in"))
        sdec_filled = sem("sdec_filled")
        kx_in = [sem(f"kx_in{s}") for s in range(4)]
        kx_turned, kxt_a, kxt_d, dix_done, dix_read, dix_red = (sem(x) for x in (
            "kx_turned", "kxt_by_act", "kxt_by_dve", "dix_done", "dix_read", "dix_reduced"))
        ix_done, ix_relu, ix_acc, ix_causal = sem("ix_done"), sem("ix_relu"), sem("ix_acc"), sem("ix_causal")
        dcmp_done, dcnt_done, dcnt_read = sem("dcmp_done"), sem("dcnt_done"), sem("dcnt_read")
        fin_a, fin_a_mm, fin_b, fin_b_mm, fin_c, fin_c_mm, fin_c_read, gidx_ready, flags_mm = (sem(x) for x in (
            "fin_eq_prefix", "fin_eq_offsets", "fin_rank_prefix", "fin_rank_offsets", "fin_onehot", "fin_slots",
            "fin_slots_read", "gather_rows_ready", "new_flags"))
        h_prep, h_lev, h_at, hq_free, hf_free = sem("h_prep"), sem("h_level"), sem("h_masked"), sem("hq_free"), sem("hf_free")
        h_mm, h_kt, h_kt_mm, h_ktok, h_u, h_state, h_o, h_osq, h_ss, h_sd, h_orow = (sem(x) for x in (
            "h_level_mm", "h_tails", "h_turned", "h_ktok", "h_update", "h_state", "h_out_mm", "h_squared", "h_ss", "h_sd", "h_out"))
        rg_ready, ri_out, q_out, sp_out, ss_out = sem("rg_ready"), sem("ri_scratch"), sem("q_scratch"), sem("state_prompt_out"), sem("state_sample_out")
        kvout = sem("kv_out")
        at_qk, at_sm, at_exp, at_tr, at_ptc, at_pv, at_on, at_ott, at_otc = (sem("at_" + x) for x in (
            "logits", "max", "exp", "turned", "pt", "pv", "normed", "out_turned", "out_copied"))
        bias_ready = sem("bias_ready")
        qd_zero, qd_in, vn_in, s0_in, vb_in = sem("qd_zeroed"), sem("qd_in"), sem("vn_in"), sem("s0_in"), sem("vb_in")
        ks_in, d_kt, d_ktc, d_qk, d_sub, d_exp, d_p, d_pt, d_ptc, d_pv, d_od = (sem("dec_" + x) for x in (
            "kv_in", "k_turned", "kt_copied", "logits", "centred", "exp", "probs", "p_turned", "p_copied", "pv", "out"))
        o_out, oa_in, ds_new, ds_prod, ds_mm, or2_ready, or_out, or_in, ds_ss, ds_sd, od8_ready, od8_mm, ot_ready = (sem("dec_" + x) for x in (
            "o_scratch", "o_in", "state_new", "state_prod", "state_mm", "or2", "or_scratch", "or_in", "ss", "sd", "od8", "od8_turned", "ot_ready"))
        otr_mm, otr_copied = sem("otr_turned"), sem("otr_copied")

        UNITS = [("f", "qi", 0 + j // 2, j % 2, tg, j) for j in range(4) for tg in range(TG)]
        UNITS += [("t", "kv", 2, 256, b, 0) for b in range(9)] + [("t", "kiw", 3, 72, b, 0) for b in range(9)]
        N1 = len(UNITS)
        UNITS += [("f", "q", 4 + j // 2, j % 2, tg, j) for j in range(4) for tg in range(TG)]
        UNITS += [("t", "ri", 6 + j, 256, b, j) for j in range(2) for b in range(9)]
        NRI = len(UNITS)
        UNITS += [("t", "rg", 8 + j, 256, b, j) for j in range(2) for b in range(9)]
        N2 = len(UNITS)
        for t in range(4):
            UNITS += [("f", ("rf", "rq")[j], 10 + t, j, tg, t) for j in range(2) for tg in range(TG)]
        NBITS = 32
        EARLY = 4
        LOOPED = NBITS - 3 * EARLY

        def steps():
            return [(b, h) for b in range(BLK - 1, -1, -1) for h in range(H)]
        STEPS = steps()
        NPASS = 8

        def halves(x, h):
            v = x.rearrange("p (n s h) -> p n s h", s=2, h=h)
            return v[:, :, 0, :], v[:, :, 1, :]

        def pool_consts(pool, G, link):
            link(G.memset(HALF1[:, :], 0.0))
            link(G.memset(HALF1[0:64, 0:64], 1.0))
            link(G.memset(HALF1[64:P, 64:P], 1.0))
            link(G.memset(TRI[:, :], 1.0))
            link(G.affine_select(out=TRI[:, :], in_=TRI[:, :], compare_op=ALU.is_gt, fill=0.0, base=0,
                                 pattern=[[1, P]], channel_multiplier=-1))
            link(G.tensor_copy(AUX[:, 384:512], TRI[:, :]))
            link(G.memset(TRI[0:64, 64:P], 0.0))
            link(G.memset(CAUSAL[:, :], 0.0))
            link(G.affine_select(out=CAUSAL[:, P:2 * P], in_=CAUSAL[:, P:2 * P], compare_op=ALU.is_ge, fill=-MASKED,
                            base=0, pattern=[[-1, P]], channel_multiplier=1))
            link(G.memset(ROW63[:, :, :], 0.0))
            for half in range(2):
                link(G.affine_select(out=ROW63[:, half, :], in_=ROW63[:, half, :], compare_op=ALU.not_equal, fill=1.0,
                                base=-(63 + 64 * half), pattern=[[0, NB]], channel_multiplier=1))
            link(G.iota(IOTA[:, :], [[1, TOPK]], base=1, channel_multiplier=0, allow_small_or_imprecise_dtypes=True))
            link(G.iota(SLOT[:, :], [[P, 2]], base=1, channel_multiplier=1, allow_small_or_imprecise_dtypes=True))
            link(G.iota(AUX[:, 0:P].bitcast(i32), [[0, P]], base=0, channel_multiplier=1))
            link(G.iota(AUX[:, P:2 * P].bitcast(i32), [[1, P]], base=0, channel_multiplier=0))
            link(G.memset(BITS[:, 0:1].bitcast(i32), -1))
            for i in range(31):
                link(G.memset(BITS[:, 1 + i:2 + i], 1 << (30 - i)))
            G.memset(BITS[:, 32:33], 0).then_inc(maps_built, 1)
            with nc.allow_non_contiguous_dma(reason="page ids and bounds, one element per partition"):
                pool.dma_start(PGI[:, :], I["page_table"].rearrange("(g h) n -> (h n) g", h=2)).then_inc(pages_in, 16)
                for r in range(2):
                    pool.dma_start(LB[:, r, :], I["hgrn_lb"][r].rearrange("(t p) -> p t", p=P)).then_inc(lb_in, 16)
                pool.dma_start(NORMG[:, :], I["hgrn_norm_g"][0:1, :].to_broadcast([P, 512])).then_inc(lb_in, 16)

        def pool_mixer(pool, G, link):
            kidx_rows = I["cache_kidx"][0].rearrange("n (s k) d -> (n s) (k d)", k=16)

            def gather_keys(r):
                gp, sub = divmod(r, 8)
                if r >= 4:
                    pool.wait_ge(kx_turned, r - 3)
                pool.indirect_dma_start(KX[:, r % 4, :], None, kidx_rows,
                                        bass.IndirectOffsetOnAxis(ap=PGX[:, sub, gp:gp + 1], axis=0),
                                        bounds_check=NPHYS * 8 - 1, oob_is_err=False).then_inc(kx_in[r % 4], 16)
            pool.wait_ge(pgx_ready, 1)
            for r in range(4):
                gather_keys(r)
            G.memset(SDECF, NEG).then_inc(sdec_filled, 1)
            G.memset(QB[:, :, :, :], 0.0).then_inc(qb_zero, 1)
            nc_ok = nc.allow_non_contiguous_dma(reason="eight sample columns")
            with nc_ok:
                pool.wait_ge(unit_out, 12)
                pool.dma_start(qi_s.rearrange("(t p) b -> p t b", p=P), QIT[:, :, SEQ:TOK]).then_inc(qi_out, 16)
                pool.wait_ge(qi_out, 16)
                pool.wait_ge(qb_zero, 1)
                for par in range(2):
                    pool.dma_start(QB[64 * par:64 * par + 64, par, :, :],
                                   qi_s.rearrange("(h d) b -> d h b", d=HD)).then_inc(qb_in, 16)
                pool.wait_ge(wis_ready, 1)
                pool.dma_start(w_s, WIS[0:NB, 8, :]).then_inc(w_outd, 16)
                pool.wait_ge(w_outd, 16)
                for half in range(2):
                    src = w_s.rearrange("(g u) h -> u g h", u=2)[half:half + 1].to_broadcast([64, 4, H])
                    pool.dma_start(WDEC[64 * half:64 * half + 64, :, :], src).then_inc(w_in_dec, 16)
                pool.wait_ge(unit_out, N1)
                for name, c in (("k_", 0), ("v_", P)):
                    pool.dma_start(O[name + "prompt"][0, 0].rearrange("(b p) g d -> p b (g d)", p=P),
                                   KV[:, 0:BLK, c:c + P]).then_inc(kvout, 16)
                    pool.dma_start(O[name + "sample"][0, :, 0].rearrange("b g d -> b (g d)"),
                                   KV[0:NB, 8, c:c + P]).then_inc(kvout, 16)
                pool.dma_start(O["kidx_prompt"][0, 0].rearrange("(b p) d -> p b d", p=P),
                               KIW[:, 0:BLK, 0:HD]).then_inc(kvout, 16)
                pool.dma_start(O["kidx_sample"][0, :, 0], KIW[0:NB, 8, 0:HD]).then_inc(kvout, 16)
                pool.wait_ge(sn_ready, 1)
                pool.dma_start(sn_s, SN).then_inc(sn_out, 16)
                pool.wait_ge(sn_out, 16)
                pool.wait_ge(sdec_filled, 1)
                for half in range(2):
                    row = 64 * half + 63
                    pool.dma_start(SDEC[row:row + 1, :, PAGE:PAGE + 1],
                                   sn_s.rearrange("(g u) o -> u g o", u=2)[half:half + 1]).then_inc(sn_in, 16)
                for r in range(4, 32):
                    gather_keys(r)
                for b in range(FIRST_TOPK, BLK):
                    pool.wait_ge(ix_acc, 8 * (b - 1))
                    s = score(b)[:, P * b:P * b + P]
                    G.affine_select(out=s, in_=s, compare_op=ALU.is_ge, fill=NEG, base=0, pattern=[[-1, P]],
                                    channel_multiplier=1).then_inc(ix_causal, 1)
                pool.wait_ge(unit_out, NRI)
                pool.dma_start(q_s.rearrange("(t p) b -> p t b", p=P), QT[:, :, SEQ:TOK]).then_inc(q_out, 16)
                pool.dma_start(ri_s, RIS).then_inc(ri_out, 16)
                pool.wait_ge(unit_out, N2)
                for b in range(9):
                    rows = P if b < BLK else NB
                    G.tensor_tensor(RG[0:rows, b, :], RG[0:rows, b, :], NORMG[0:rows, :], ALU.mult).then_inc(rg_ready, 1)
                for t in range(4):
                    pool.wait_ge(h_state, BLK * (t + 1))
                    pool.dma_start(O["state_prompt"][0, 0, 2 * t:2 * t + 2].rearrange("h d e -> (h d) e"),
                                   SC[:, BLK, :]).then_inc(sp_out, 16)
                    pool.wait_ge(sp_out, 16 * t + 16)
                pool.wait_ge(gidx_ready, 1)
                pool.wait_ge(h_o, 4)
                pool.wait_ge(ri_out, 16)
                for j in range(16):
                    for name, dst in (("cache_k", KS), ("cache_v", VS)):
                        pool.indirect_dma_start(dst[:, j, :], None, I[name][0].rearrange("n k g d -> (n k) (g d)"),
                                                bass.IndirectOffsetOnAxis(ap=GIDX[:, j:j + 1], axis=0),
                                                bounds_check=NPHYS * PAGE - 1, oob_is_err=False).then_inc(ks_in, 16)
                pool.wait_ge(kvout, 16 * 6)
                pool.dma_start(VN, O["v_sample"][0, :, 0].rearrange("(o b) g d -> o b (g d)", o=1)).then_inc(vn_in, 16)
                pool.wait_ge(at_otc, BLK)
                link(G.memset(QD[:, :, :], 0.0))
                pool.wait_ge(q_out, 16)
                for g in range(GRP):
                    pool.dma_start(QD[64 * g:64 * g + 64, 4 * g:4 * g + 4, :],
                                   q_s.rearrange("(h d) b -> d h b", d=HD)[:, 4 * g:4 * g + 4, :]).then_inc(qd_in, 16)
                for t in range(4):
                    pool.dma_start(S0[:, t], I["state_hgrn"][0, :, 2 * t:2 * t + 2].rearrange("b h d e -> (h d) b e"))\
                        .then_inc(s0_in, 16)
                for t in range(4):
                    for half in range(2):
                        c = HD * (2 * t + half)
                        src = ri_s[:, c:c + HD].rearrange("(o b) e -> o b e", o=1).to_broadcast([64, NB, HD])
                        pool.dma_start(VB[64 * half:64 * half + 64, t], src).then_inc(vb_in, 16)
                pool.wait_ge(ds_new, 1)
                for t in range(4):
                    pool.dma_start(O["state_sample"][0, :, 2 * t:2 * t + 2].rearrange("b h d e -> (h d) b e"), T1[:, t])\
                        .then_inc(ss_out, 16)
                pool.wait_ge(d_od, 1)
                for g in range(GRP):
                    pool.dma_start(o_s.rearrange("b (h d) -> h b d", d=HD)[4 * g:4 * g + 4],
                                   OD[4 * g:4 * g + 4, :, HD * g:HD * g + HD]).then_inc(o_out, 16)
                pool.wait_ge(or2_ready, 1)
                for t in range(4):
                    pool.dma_start(or_s.rearrange("b (t h e) -> t h b e", t=4, h=2)[t], OR2[:, t]).then_inc(or_out, 16)
                pool.wait_ge(o_out, 32)
                pool.dma_start(OD8[:, 0:512], o_s).then_inc(oa_in, 16)
                pool.wait_ge(or_out, 64)
                pool.dma_start(OD8[:, 512:1024], or_s).then_inc(or_in, 16)
                pool.wait_ge(ss_out, 64)
                pool.wait_ge(oa_in, 16)
                pool.wait_ge(or_in, 16)

        def pe_mixer(pe, cols, norm_stats):
            T, M = nc.tensor.transpose, nc.tensor.matmul
            loaded = [0]

            def unit(u):
                kind, name, m, a, x, _ = UNITS[u]
                n = MIX0 + m
                if u == 0 or UNITS[u - 1][2] != m:
                    pe.wait_ge(ring_in[n % 4], reach[n])
                if u >= 3:
                    pe.wait_ge(unit_out, u - 2)
                for k in range(DT):
                    if kind == "f":
                        w = RING[:, n % 4, :].rearrange("p (k c) -> p k c", c=SLAB)
                        last = M(PS[:, u % 3, 0:TW], w[:, k, P * a:P * a + P], ACTS[:, k, cols(x)],
                                 start=k == 0, stop=k == DT - 1)
                    else:
                        rows = P if x < BLK else NB
                        w = RING[:, n % 4, 0:DT * a].rearrange("p (k c) -> p k c", c=a)
                        last = M(PS[0:rows, u % 3, 0:a], ACTS[:, k, P * x:P * x + rows], w[:, k, :],
                                 start=k == 0, stop=k == DT - 1)
                last.then_inc(unit_done, 1)

            for u in range(N1):
                unit(u)
            for b in range(9):
                rows = P if b < BLK else NB
                if b >= 2:
                    pe.wait_ge(k3_ready, b - 1)
                pe.wait_ge(kd_ready, b + 1)
                for i in range(3):
                    last = T(PS[:, 4 + b % 2, P * i:P * i + rows], KD[0:rows, b % 2, P * i:P * i + P], IDENT[0:rows, 0:rows])
                last.then_inc(k_turned, 1)
            for j in range(4):
                last = T(PS[0:NB, 6, P * j:P * j + P], QIT[:, j, SEQ:TOK], IDENT[:, :])
            last.then_inc(qid_turned, 1)

            def turn_keys(r):
                pe.wait_ge(kx_in[r % 4], 16 * (r // 4 + 1))
                if r >= 2:
                    pe.wait_ge(kxt_a, r - 1)
                    pe.wait_ge(kxt_d, r - 1)
                for j in range(8):
                    last = T(PS[:, 2 * (r % 2) + j // 4, P * (j % 4):P * (j % 4) + P], KX[:, r % 4, P * j:P * j + P], IDENT[:, :])
                last.then_inc(kx_turned, 1)

            def key_logits(r):
                gp = r // 8
                pe.wait_ge(kxt_a, r + 1)
                pe.wait_ge(kxt_d, r + 1)
                if r >= 2:
                    pe.wait_ge(dix_read, 2 * r - 2)
                for j in range(8):
                    last = M(PS[:, 6 + r % 2, 32 * j:32 * j + 32], KXT[:, r % 2, P * j:P * j + P],
                             QB[:, :, :, 2 * gp:2 * gp + 2], start=True, stop=True)
                last.then_inc(dix_done, 1)
            pe.wait_ge(k3_ready, 9)
            pe.wait_ge(qb_in, 32)
            pe.wait_ge(sn_ready, 1)
            pe.wait_ge(unit_out, N1)
            turn_keys(0)
            for r in range(32):
                if r + 1 < 32:
                    turn_keys(r + 1)
                key_logits(r)
            pe.wait_ge(dix_read, 64)
            for i in range(6 * H):
                b, h = divmod(i, H)
                b += FIRST_TOPK
                if i >= 2:
                    pe.wait_ge(ix_relu, i - 1)
                rows = slice(64 * (h % 2), 64 * (h % 2) + 64)
                n = P * (b + 1)
                for c in range(0, n, 512):
                    last = M(PS[:, 4 + 2 * (i % 2) + c // 512, 0:min(512, n - c)], QIT[rows, h // 2, P * b:P * b + P],
                             K3[rows, 2, c:min(c + 512, n)], start=True, stop=True)
                last.then_inc(ix_done, 1)
            pe.wait_ge(ix_relu, 6 * H)
            def count(i):
                pe.wait_ge(dcmp_done, i + 1)
                M(PS[:, 3, 0:4], HALF1[:, :], DCNT, start=True, stop=True).then_inc(dcnt_done, 1)

            for i in range(N2 - N1):
                unit(N1 + i)
                if i % 2 == 0 and i // 2 < LOOPED:
                    count(i // 2)
            for u in range(N2, N2 + 6):
                unit(u)

            def select():
                pe.wait_ge(fin_a, 1)
                M(PS[:, 5, 0:4], HALF1[:, :], GTC, start=True, stop=True)
                M(PS[:, 5, 8:12], TRI[:, :], DRK.rearrange("p (g k) -> p g k", k=PAGE + 1)[:, :, PAGE], start=True, stop=True)\
                    .then_inc(fin_a_mm, 1)
                for u in range(N2 + 18, N2 + 21):
                    unit(u)
                pe.wait_ge(fin_b, 1)
                M(PS[:, 6, 0:4], TRI[:, :], DRK.rearrange("p (g k) -> p g k", k=PAGE + 1)[:, :, PAGE], start=True, stop=True)
                for half in range(2):
                    last = M(PS[0:H, 7, 4 * half:4 * half + 4], ROW63[:, half, :],
                             DGT.rearrange("p (g k) -> p g k", k=PAGE + 1)[:, :, PAGE], start=True, stop=True)
                last.then_inc(fin_b_mm, 1)
                for u in range(N2 + 21, N2 + 24):
                    unit(u)
                for gp in range(4):
                    pe.wait_ge(fin_c, gp + 1)
                    if gp >= 2:
                        pe.wait_ge(fin_c_read, gp - 1)
                    for sh in range(2):
                        for half in range(2):
                            rows = slice(64 * half, 64 * half + 64)
                            last = M(PS[:, 4 + 2 * (gp % 2) + half, 129 * sh:129 * sh + 129],
                                     DONE_HOT[rows, gp, P * sh:P * sh + P], DRANK[rows, gp, :], start=True, stop=True)
                    last.then_inc(fin_c_mm, 1)
                pe.wait_ge(fin_c_read, 4)

            for t in range(4):
                if t < 3:
                    for j in range(6):
                        if t < 2:
                            unit(N2 + 6 * (t + 1) + j)
                        if j % 3:
                            count(LOOPED + EARLY * t + j - 1 - j // 3)
                for lv in range(NPASS):
                    if lv == 0:
                        pe.wait_ge(h_prep, t + 1)
                        if t:
                            pe.wait_ge(h_orow, t)
                    else:
                        pe.wait_ge(h_lev, 7 * t + lv)
                    for hd in range(2):
                        n = 2 * (NPASS * t + lv) + hd
                        if n >= 2:
                            pe.wait_ge(h_at, n - 1)
                        rows = slice(64 * hd, 64 * hd + 64)
                        for c in range(BLK):
                            k = (HK if lv == 0 else LV[:, lv % 2])[rows, P * c:P * c + P]
                            q = (HQ if lv == 0 else LV[:, lv % 2])[rows, P * c:P * c + P]
                            last = M(PS[:, 4 + 2 * hd + c // 4, P * (c % 4):P * (c % 4) + P], k, q, start=True, stop=True)
                        last.then_inc(h_mm, 1)
                pe.wait_ge(h_kt, t + 1)
                pe.wait_ge(h_at, 2 * NPASS * (t + 1))
                for c in range(BLK):
                    last = T(PS[:, 4 + c // 4, P * (c % 4):P * (c % 4) + P], LV[:, 0, P * c:P * c + P], IDENT[:, :])
                last.then_inc(h_kt_mm, 1)
                pe.wait_ge(h_ktok, t + 1)
                for c in range(BLK):
                    last = M(PS[:, 6 + c // 4, P * (c % 4):P * (c % 4) + P], KTOK[:, c, :], RI[:, c, P * t:P * t + P],
                             start=True, stop=True)
                last.then_inc(h_u, 1)
                for c in range(BLK):
                    if c:
                        pe.wait_ge(h_state, BLK * t + c)
                    for hd in range(2):
                        rows = slice(64 * hd, 64 * hd + 64)
                        out = PS[:, 4 + hd, HD * c:HD * c + HD]
                        e0 = P * t + HD * hd
                        last = M(out, AT[:, hd, c, :], RI[:, c, e0:e0 + HD], start=True, stop=c == 0)
                        if c:
                            last = M(out, LV[rows, 1, P * c:P * c + P], SC[rows, c, :], start=False, stop=True)
                last.then_inc(h_o, 1)
                if t == 2:
                    select()

            pe.wait_ge(h_orow, 4)

            def qk(i):
                b, h = STEPS[i]
                if i >= 2:
                    pe.wait_ge(at_sm, i - 1)
                rows = slice(64 * (h % 2), 64 * (h % 2) + 64)
                n = P * (b + 1)
                for c in range(0, n, 512):
                    last = M(PS[:, 4 + 2 * (i % 2) + c // 512, 0:min(512, n - c)], QT[rows, h // 2, P * b:P * b + P],
                             K3[rows, h // 4, c:min(c + 512, n)], start=True, stop=True)
                last.then_inc(at_qk, 1)

            def turn_probs(i):
                b, _ = STEPS[i]
                pe.wait_ge(at_exp, i + 1)
                if i:
                    pe.wait_ge(at_ptc, i)
                for j in range(b + 1):
                    last = T(PS[:, j // 4, P * (j % 4):P * (j % 4) + P], SM[:, i % 2, P * j:P * j + P], IDENT[:, :])
                last.then_inc(at_tr, 1)

            def pv(i):
                b, h = STEPS[i]
                pe.wait_ge(at_ptc, i + 1)
                if h == 0 and i:
                    pe.wait_ge(at_on, i // H)
                for j in range(b + 1):
                    c = P + HD * (h // 4)
                    last = M(PS[:, 2, HD * h:HD * h + HD], PT[:, i % 2, P * j:P * j + P], KV[:, j, c:c + HD],
                             start=j == 0, stop=j == b)
                last.then_inc(at_pv, 1)

            def turn_out_rows(bi):
                pe.wait_ge(at_on, bi + 1)
                if bi:
                    pe.wait_ge(at_otc, bi)
                for j in range(4):
                    last = T(PS[:, 3, P * j:P * j + P], OTOK[:, bi % 2, P * j:P * j + P], IDENT[:, :])
                last.then_inc(at_ott, 1)
            qk(0)
            for i in range(64):
                if i + 1 < 64:
                    qk(i + 1)
                turn_probs(i)
                if i:
                    pv(i - 1)
                if i >= H and i % H == 2:
                    turn_out_rows(i // H - 1)
            pv(63)
            turn_out_rows(7)

            pe.wait_ge(ks_in, 16 * 32)
            pe.wait_ge(at_sm, 64)
            for a in range(4):
                for j in range(4):
                    last = T(PS[:, 4 + a, P * j:P * j + P], KS[:, 4 * a + j, :], IDENT[:, :])
                last.then_inc(d_kt, 1)
            pe.wait_ge(ds_prod, 1)
            pe.wait_ge(at_otc, BLK)
            for t in range(4):
                last = M(PS[0:2, t, :], HALF1[:, 0:P:64], T2[:, t], start=True, stop=True)
            last.then_inc(ds_mm, 1)
            pe.wait_ge(d_ktc, 6)
            pe.wait_ge(qd_in, 32)
            pe.wait_ge(or2_ready, 1)
            for b in range(NB):
                last = M(PS[0:H, b, 0:TOPK + 1], QD[:, :, b], KTD[:, b, :], start=True, stop=True)
            last.then_inc(d_qk, 1)
            pe.wait_ge(d_p, 1)
            for b in range(NB):
                for half in range(2):
                    j = 2 * b + half
                    T(PS[:, 4, H * j:H * j + H], SDD[:, b, P * half:P * half + P], IDENT[0:H, 0:H])
                last = T(PS[0:1, 5, H * b:H * b + H], SDD[:, b, TOPK:TOPK + 1], IDENT[0:H, 0:H])
            last.then_inc(d_pt, 1)
            pe.wait_ge(d_ptc, 2)
            pe.wait_ge(vn_in, 16)
            for b in range(NB):
                out = PS[0:H, 6 + b // 4, P * (b % 4):P * (b % 4) + P]
                for half in range(2):
                    M(out, PTD[:, 2 * b + half, :], VS[:, 2 * b + half, :], start=half == 0, stop=False)
                last = M(out, PTN[:, b, :], VN[:, b, :], start=False, stop=True)
            last.then_inc(d_pv, 1)
            for b in range(BLK):
                if b >= 4:
                    pe.wait_ge(otr_copied, b - 3)
                for j in range(4):
                    last = T(PS[:, b % 4, P * j:P * j + P], RG[:, b, P * j:P * j + P], IDENT[:, :])
                last.then_inc(otr_mm, 1)
            pe.wait_ge(od8_ready, 1)
            pe.wait_ge(d_ptc, 2)
            for k in range(DT):
                last = T(PS[:, 4, NB * k:NB * k + NB], OD8[:, P * k:P * k + P], IDENT[0:NB, 0:NB])
            last.then_inc(od8_mm, 1)
            pe.wait_ge(ot_ready, 2)
            pe.wait_ge(otr_copied, BLK)
            for d in range(DT):
                n = MIX0 + 14 + d // 2
                if d % 2 == 0:
                    pe.wait_ge(ring_in[n % 4], reach[n])
                w = RING[:, n % 4, :].rearrange("p (k c) -> p k c", c=SLAB)
                for tg in range(TG):
                    if d >= 2:
                        pe.wait_ge(z_done, 24 + 3 * d + tg + 1 - 6)
                    elif d == 1 and tg == 0:
                        pe.wait_ge(d_od, 1)
                    for k in range(DT):
                        src = OTA[:, k, cols(tg)] if k < 4 else OTR[:, k - 4, cols(tg)]
                        last = M(PS[:, 3 * (d % 2) + tg, 0:TW], w[:, k, P * (d % 2):P * (d % 2) + P], src,
                                 start=k == 0, stop=k == DT - 1)
                    last.then_inc(y_done, 1)
            norm_stats(1)

        def act_mixer(act, A, link):
            act.wait_ge(lb_diff, 1)
            A(LB[:, 2, :], LB[:, 2, :], ACT.Sigmoid).then_inc(lb_sig, 1)

            def unit(u):
                kind, name, m, a, x, j = UNITS[u]
                act.wait_ge(unit_done, u + 1)
                rows = P if kind == "f" or x < BLK else NB
                width = TW if kind == "f" else a
                src = PS[0:rows, u % 3, 0:width]
                cols = slice(TW * x, TW * x + TW)
                func, scale = ACT.Copy, 1.0
                if name == "qi":
                    dst = QIT[:, j, cols]
                elif name == "kv":
                    dst = KV[0:rows, x, :]
                elif name == "kiw":
                    dst = KIW[0:rows, x, :]
                elif name == "q":
                    dst, scale = QT[:, j, cols], KSCALE
                elif name == "ri":
                    dst = RI[:, x, 256 * j:256 * j + 256] if x < BLK else RIS[:, 256 * j:256 * j + 256]
                elif name == "rg":
                    dst, func = RG[0:rows, x, 256 * j:256 * j + 256], ACT.Silu
                elif name == "rf":
                    if j and x == 0:
                        act.wait_ge(hf_free, j)
                    dst, func = HF[:, cols], ACT.Sigmoid
                else:
                    if j and x == 0:
                        act.wait_ge(hq_free, j)
                    dst = HQ[:, cols]
                A(dst, src, func, scale=scale).then_inc(unit_out, 1)
            for u in range(N1):
                unit(u)
            act.wait_ge(unit_out, N1)
            A(WIS[:, 0:BLK, :], KIW[:, 0:BLK, HD:HD + H], ACT.Copy, scale=H ** -0.5)
            A(WIS[0:NB, BLK, :], KIW[0:NB, BLK, HD:HD + H], ACT.Copy, scale=H ** -0.5).then_inc(wis_ready, 1)
            for r in range(32):
                act.wait_ge(kx_turned, r + 1)
                if r >= 2:
                    act.wait_ge(dix_done, r - 1)
                A(KXT[:, r % 2, 0:512], PS[:, 2 * (r % 2), :], ACT.Copy).then_inc(kxt_a, 1)
            for i in range(6 * H):
                n = P * (FIRST_TOPK + i // H + 1)
                act.wait_ge(ix_done, i + 1)
                if i >= 2:
                    act.wait_ge(ix_acc, i - 1)
                src = PS[:, 4 + 2 * (i % 2):6 + 2 * (i % 2), :].rearrange("p u c -> p (u c)")[:, 0:n]
                A(RELU[:, i % 2, 0:n], src, ACT.Relu, scale=KSCALE).then_inc(ix_relu, 1)
            for u in range(N1, N2 + 6):
                if UNITS[u][1] == "rg" and UNITS[u - 1][1] == "ri":
                    act.wait_ge(ix_acc, 6 * H)
                    act.wait_ge(sn_ready, 1)
                unit(u)
            for t in range(4):
                if t < 2:
                    for u in range(N2 + 6 * (t + 1), N2 + 6 * (t + 1) + 3):
                        unit(u)
                act.wait_ge(h_kt_mm, t + 1)
                A(KTOK[:, :, :].rearrange("p (u c) x -> p u (c x)", u=2), PS[:, 4:6, :], ACT.Copy).then_inc(h_ktok, 1)
                if t < 2:
                    for u in range(N2 + 6 * (t + 1) + 3, N2 + 6 * (t + 2)):
                        unit(u)
                act.wait_ge(h_o, t + 1)
                A(OSQ.rearrange("p (u c) -> p u c", u=2), PS[:, 4:6, :], ACT.Square).then_inc(h_osq, 1)
                act.wait_ge(h_ss, t + 1)
                A(SR, SS, ACT.Sqrt, scale=1.0 / HD, bias=EPS[:, 2:3]).then_inc(h_sd, 1)
                if t == 2:
                    for u in range(N2 + 18, N2 + 24):
                        unit(u)

            def expo(i):
                b, h = STEPS[i]
                act.wait_ge(at_sm, i + 1)
                if h == 0 and i >= 2 * H:
                    act.wait_ge(at_on, i // H - 1)
                s = SM[:, i % 2, 0:P * (b + 1)]
                A(s, s, ACT.Exp, bias=NMX[:, i % 2:i % 2 + 1], accum_out=SUMS[:, (i // H) % 2, h:h + 1])\
                    .then_inc(at_exp, 1)

            def copy(i):
                b, h = STEPS[i]
                n = P * (b + 1)
                act.wait_ge(at_tr, i + 1)
                if i >= 2:
                    act.wait_ge(at_pv, i - 1)
                A(PT[:, i % 2, 0:n], PS[:, 0:2, :].rearrange("p u c -> p (u c)")[:, 0:n], ACT.Copy).then_inc(at_ptc, 1)

            def out_rows(bi):
                b = BLK - 1 - bi
                act.wait_ge(at_ott, bi + 1)
                A(OTA[:, :, P * b:P * b + P], PS[:, 3, :].rearrange("p (k t) -> p k t", t=P), ACT.Copy).then_inc(at_otc, 1)
            expo(0)
            for i in range(64):
                if i + 1 < 64:
                    expo(i + 1)
                copy(i)
                if i >= H and i % H == 2:
                    out_rows(i // H - 1)
            out_rows(7)
            for a in range(4):
                act.wait_ge(d_kt, a + 1)
                A(KTD[:, 2 * a:2 * a + 2, 0:TOPK], PS[:, 4 + a, :].rearrange("p (b c) -> p b c", c=TOPK), ACT.Copy)\
                    .then_inc(d_ktc, 1)
            act.wait_ge(ds_mm, 1)
            A(OR2.rearrange("p t b e -> p t (b e)"), PS[0:2, 0:4, :], ACT.Copy).then_inc(or2_ready, 1)
            act.wait_ge(d_sub, 1)
            A(SDD, SDD, ACT.Exp).then_inc(d_exp, 1)
            act.wait_ge(d_pv, 1)
            A(OD.rearrange("p (u b) c -> p u (b c)", u=2), PS[0:H, 6:8, :], ACT.Copy).then_inc(d_od, 1)
            for b in range(BLK):
                act.wait_ge(otr_mm, b + 1)
                A(OTR[:, :, P * b:P * b + P], PS[:, b % 4, :].rearrange("p (k t) -> p k t", t=P), ACT.Copy).then_inc(otr_copied, 1)
            act.wait_ge(ds_ss, 1)
            A(DSS, DSS, ACT.Sqrt, scale=1.0 / HD, bias=EPS[0:NB, 2:3]).then_inc(ds_sd, 1)

        def dve_consts(dve, V, link):
            dve.wait_ge(maps_built, 1)
            bits = AUX[:, 256:384].bitcast(i32)
            link(V.tensor_tensor(bits, AUX[:, 0:P].bitcast(i32), AUX[:, P:2 * P].bitcast(i32), ALU.bitwise_xor))
            sh, eq = AUX[:, 512:640].bitcast(i32), AUX[:, 640:768]
            for lv in range(7):
                link(V.tensor_scalar(sh, bits, lv, None, ALU.logical_shift_right))
                link(V.tensor_scalar(eq, sh, 1.0, None, ALU.is_equal))
                link(V.tensor_tensor(LEVELS[:, lv, :], eq, AUX[:, 384:512], ALU.mult))
            dve.wait_ge(pages_in, 16)
            pf = PG[:, 0:4]
            link(V.tensor_scalar(pf, PGI[:, :], 8.0, None, ALU.mult))
            for s in range(8):
                last = V.tensor_scalar(PGX[:, s, :], pf, float(s), None, ALU.add)
            last.then_inc(pgx_ready, 1)
            dve.wait_ge(lb_in, 48)
            V.tensor_tensor(LB[:, 2, :], LB[:, 0, :], LB[:, 1, :], ALU.subtract).then_inc(lb_diff, 1)

        def dve_mixer(dve, V, link, step, residual, norm):
            dve.wait_ge(lb_sig, 1)
            V.tensor_scalar(LB[:, 3, :], LB[:, 2, :], -1.0, 1.0, ALU.mult, ALU.add).then_inc(lb_ready, 1)
            def turned(b):
                rows = P if b < BLK else NB
                dve.wait_ge(k_turned, b + 1)
                V.tensor_copy(K3[:, :, P * b:P * b + rows],
                              PS[:, 4 + b % 2, 0:3 * P].rearrange("p (g t) -> p g t", t=P)[:, :, 0:rows]).then_inc(k3_ready, 1)
            for b in range(9):
                rows = P if b < BLK else NB
                dve.wait_ge(unit_out, 12 + 9 + b + 1)
                if b >= 2:
                    dve.wait_ge(k_turned, b - 1)
                V.tensor_copy(KD[0:rows, b % 2, 0:2 * P].rearrange("p (g u d) -> p g u d", g=2, u=2),
                              KV[0:rows, b, 0:P].rearrange("p (g d) -> p g d", g=2).unsqueeze(2).to_broadcast([rows, 2, 2, HD]))
                V.tensor_copy(KD[0:rows, b % 2, 2 * P:3 * P].rearrange("p (u d) -> p u d", u=2),
                              KIW[0:rows, b, 0:HD].unsqueeze(1).to_broadcast([rows, 2, HD])).then_inc(kd_ready, 1)
                if b == 0:
                    continue
                turned(b - 1)
            turned(8)
            dve.wait_ge(qid_turned, 1)
            link(V.tensor_copy(QITOK.rearrange("p h d -> p (h d)"), PS[0:NB, 6, :]))
            link(V.tensor_tensor(QIPROD, QITOK, KIW[0:NB, 8:9, 0:HD].to_broadcast([NB, H, HD]), ALU.mult))
            link(V.tensor_reduce(DL, QIPROD, AX.X, ALU.add))
            link(V.tensor_scalar(DL, DL, KSCALE, 0.0, ALU.mult, ALU.max))
            dve.wait_ge(wis_ready, 1)
            link(V.tensor_tensor(DL, DL, WIS[0:NB, 8, :], ALU.mult))
            V.tensor_reduce(SN, DL, AX.X, ALU.add).then_inc(sn_ready, 1)
            dve.wait_ge(w_in_dec, 32)
            dve.wait_ge(sdec_filled, 1)
            link(V.tensor_scalar(WDEC, WDEC, KSCALE, None, ALU.mult))

            def reduce_keys(r):
                gp, sub = divmod(r, 8)
                dve.wait_ge(dix_done, r + 1)
                for half in range(2):
                    rows = slice(64 * half, 64 * half + 64)
                    ps = PS[rows, 6 + r % 2, 0:256].rearrange("p (k h s) -> p k h s", h=H, s=2)[:, :, :, half]
                    V.scalar_tensor_tensor(DPROD[rows, r % 2, :].rearrange("p (k h) -> p k h", h=H), ps, 0.0,
                                           WDEC[rows, gp:gp + 1, :].to_broadcast([64, 16, H]),
                                           ALU.max, ALU.mult).then_inc(dix_read, 1)
                dve.wait_ge(dix_read, 2 * r + 2)
                V.tensor_reduce(SDEC[:, gp, 16 * sub:16 * sub + 16],
                                DPROD[:, r % 2, :].rearrange("p (k h) -> p k h", h=H), AX.X, ALU.add).then_inc(dix_red, 1)
            for r in range(32):
                dve.wait_ge(kx_turned, r + 1)
                if r >= 2:
                    dve.wait_ge(dix_done, r - 1)
                V.tensor_copy(KXT[:, r % 2, 512:1024], PS[:, 2 * (r % 2) + 1, :]).then_inc(kxt_d, 1)
                if r:
                    reduce_keys(r - 1)
            reduce_keys(31)
            for i in range(6 * H):
                b, h = divmod(i, H)
                b += FIRST_TOPK
                s, r = score(b), RELU[:, i % 2, 0:P * (b + 1)]
                dve.wait_ge(ix_relu, i + 1)
                if i:
                    dve.wait_ge(ix_acc, i)
                if h == 0:
                    V.tensor_scalar(s, r, WIS[:, b, 0:1], None, ALU.mult).then_inc(ix_acc, 1)
                else:
                    V.scalar_tensor_tensor(s, r, WIS[:, b, h:h + 1], s, ALU.mult, ALU.add).then_inc(ix_acc, 1)
            link(V.memset(CAND[:, :], 0))
            dve.wait_ge(ix_causal, 6)
            dve.wait_ge(sn_in, 32)
            dve.wait_ge(dix_red, 32)
            cand = CAND[:, :].bitcast(f32)
            PER = 12

            def one_bit(i, chain):
                chain(V.tensor_tensor(DCMP, SDEC, cand[:, 6:10].unsqueeze(2).to_broadcast([P, 4, PAGE + 1]), ALU.is_ge), 1)
                V.tensor_reduce(DCNT, DCMP, AX.X, ALU.add).then_inc(dcmp_done, 1)
                for b in range(FIRST_TOPK, BLK):
                    j = b - FIRST_TOPK
                    chain(V.tensor_scalar(JUNK[:, 0:P * (b + 1)], score(b), cand[:, j:j + 1], 0.0, ALU.is_ge, ALU.add,
                                          accum_out=CNT[:, j:j + 1]), 2 + j)
                chain(V.tensor_scalar(REJ[:, 0:6].bitcast(i32), CNT[:, 0:6], float(TOPK), -1.0, ALU.is_lt, ALU.mult), 8)
                dve.wait_ge(dcnt_done, i + 1)
                chain(V.tensor_scalar(REJ[:, 6:10].bitcast(i32), PS[:, 3, 0:4], float(TOPK), -1.0, ALU.is_lt, ALU.mult), 9)
                chain(V.tensor_scalar(REJ[:, :], REJ[:, :], BITS[:, bass.ds(i, 1)], None, ALU.bitwise_and), 10)
                chain(V.tensor_tensor(CAND[:, :], CAND[:, :], REJ[:, :], ALU.bitwise_xor), 11)
                chain(V.tensor_scalar(CAND[:, :], CAND[:, :], BITS[:, bass.ds(i + 1, 1)], None, ALU.bitwise_xor), PER)

            base = step[0]
            with dve.Fori(0, LOOPED) as i:
                def chain(ins, j):
                    ins.then_inc(dve_step, 1)
                    dve.wait_ge(dve_step, PER * i + (base + j))
                one_bit(i, chain)
            step[0] += PER * LOOPED

            def select():
                th = cand[:, 6:10].unsqueeze(2).to_broadcast([P, 4, PAGE + 1])
                g3 = lambda x: x.rearrange("p (g k) -> p g k", k=PAGE + 1)
                link(V.tensor_tensor(g3(DGT), SDEC, th, ALU.is_gt))
                link(V.tensor_reduce(GTC, g3(DGT), AX.X, ALU.add))
                link(V.tensor_tensor(g3(DEQ), SDEC, th, ALU.is_equal))
                link(V.memset(RESET, 1.0))
                link(V.memset(g3(RESET)[:, :, 0:1], 0.0))
                V.tensor_tensor_scan(DRK, RESET, DEQ, 0.0, ALU.mult, ALU.add).then_inc(fin_a, 1)
                dve.wait_ge(fin_a_mm, 1)
                link(V.tensor_copy(PCC, PS[:, 5, 0:12].rearrange("p (a b) -> p a b", b=4)[:, 0:3:2, :]))
                link(V.tensor_scalar(NEED, PCC[:, 0:4], -1.0, float(TOPK), ALU.mult, ALU.add))
                link(V.tensor_tensor(NEED, NEED, PCC[:, 4:8], ALU.subtract))
                link(V.tensor_tensor(g3(DRK), g3(DRK), NEED.unsqueeze(2).to_broadcast([P, 4, PAGE + 1]), ALU.is_le))
                link(V.tensor_tensor(DRK, DRK, DEQ, ALU.mult))
                link(V.tensor_tensor(DGT, DGT, DRK, ALU.add))
                V.tensor_tensor_scan(DRK, RESET, DGT, 0.0, ALU.mult, ALU.add).then_inc(fin_b, 1)
                dve.wait_ge(fin_b_mm, 1)
                link(V.tensor_copy(EXCL, PS[:, 6, 0:4]))
                link(V.tensor_copy(NF.rearrange("p (g u) -> p u g", u=2), PS[0:H, 7, 0:8].rearrange("p (u g) -> p u g", u=2)))
                link(V.tensor_tensor(INCL, EXCL, g3(DRK)[:, :, PAGE], ALU.add))
                link(V.tensor_tensor(DRANK[:, :, 0:PAGE], g3(DRK)[:, :, 0:PAGE],
                                     EXCL.unsqueeze(2).to_broadcast([P, 4, PAGE]), ALU.add))
                link(V.tensor_copy(DRANK[:, :, PAGE], PGI[:, :]))
                for gp in range(4):
                    hot = DONE_HOT[:, gp, :]
                    link(V.tensor_scalar(hot, IOTA[:, :], EXCL[:, gp:gp + 1], None, ALU.is_gt))
                    V.scalar_tensor_tensor(hot, IOTA[:, :], INCL[:, gp:gp + 1], hot, ALU.is_le, ALU.mult).then_inc(fin_c, 1)
                for gp in range(4):
                    dve.wait_ge(fin_c_mm, gp + 1)
                    both = PS[:, 4 + 2 * (gp % 2):6 + 2 * (gp % 2), 0:258].rearrange("p u (s k) -> p u s k", k=129)
                    for sh in range(2):
                        bank = both[:, :, sh, :]
                        for half in range(2):
                            j = 2 * (2 * gp + half) + sh
                            link(V.tensor_scalar(DJUNK, bank[:, half, 0:PAGE], SLOT[:, sh:sh + 1], 0.0, ALU.is_lt, ALU.add,
                                                 accum_out=KEY[:, j:j + 1]))
                        dst = PG.rearrange("p (g u s) -> p g u s", u=2, s=2)[:, gp, :, sh]
                        last = V.tensor_copy(dst, bank[:, :, PAGE])
                        if sh == 0:
                            link(last)
                    last.then_inc(fin_c_read, 1)
                dve.wait_ge(fin_c_read, 4)
                link(V.scalar_tensor_tensor(PG, PG, float(PAGE), KEY, ALU.mult, ALU.add))
                link(V.tensor_scalar(KEY, KEY, float(PAGE), 1.0e6, ALU.is_ge, ALU.mult))
                V.tensor_tensor(GIDX[:, :], PG, KEY, ALU.add).then_inc(gidx_ready, 1)

                for b in range(FIRST_TOPK, BLK):
                    j, n, s = b - FIRST_TOPK, P * (b + 1), score(b)
                    T_ = cand[:, j:j + 1]
                    link(V.tensor_scalar(GT[:, 0:n], s, T_, 0.0, ALU.is_gt, ALU.add, accum_out=CGP[:, j:j + 1]))
                    link(V.tensor_scalar(EQ[:, 0:n], s, T_, None, ALU.is_equal))
                    link(V.tensor_scalar(NEEDP[:, j:j + 1], CGP[:, j:j + 1], -1.0, float(TOPK), ALU.mult, ALU.add))
                    link(V.tensor_tensor_scan(PRE[:, 0:n], EQ[:, 0:n], EQ[:, 0:n], 0.0, ALU.add, ALU.max))
                    link(V.scalar_tensor_tensor(EQ[:, 0:n], PRE[:, 0:n], NEEDP[:, j:j + 1], EQ[:, 0:n], ALU.is_le, ALU.mult))
                    link(V.scalar_tensor_tensor(GT[:, 0:n], GT[:, 0:n], -1.0, EQ[:, 0:n], ALU.add, ALU.add))
                    link(V.tensor_scalar(s, GT[:, 0:n], MASKED, None, ALU.mult))

            for t in range(4):
                if t == 0:
                    link(V.memset(SC[:, 0, :], 0.0))
                dve.wait_ge(unit_out, N2 + 6 * t + 3)
                link(V.tensor_scalar(HF, HF, LB[:, 3, t:t + 1], LB[:, 2, t:t + 1], ALU.mult, ALU.add))
                V.tensor_copy(PF, HF[:, 0:SEQ])
                V.tensor_copy(HD3[:, 0, t, :], HF[:, SEQ:TOK])
                link(V.tensor_scalar(HK, HF, -1.0, 1.0, ALU.mult, ALU.add))
                V.tensor_copy(HD3[:, 1, t, :], HK[:, SEQ:TOK]).then_inc(hf_free, 1)
                dve.wait_ge(unit_out, N2 + 6 * t + 6)
                V.tensor_copy(HD3[:, 2, t, :], HQ[:, SEQ:TOK]).then_inc(h_prep, 1)
                link(V.memset(SF, 1.0))

                def level(lv):
                    h = 1 << (lv - 1)
                    dst, kk, qq, pf, sf = (halves(x, h) for x in (LV[:, lv % 2], HK[:, 0:SEQ], HQ[:, 0:SEQ], PF, SF))
                    if lv >= 3:
                        dve.wait_ge(h_mm, 2 * (NPASS * t + lv - 1))
                    V.tensor_tensor(dst[0], kk[0], sf[0], ALU.mult)
                    V.tensor_tensor(dst[1], qq[1], pf[1], ALU.mult).then_inc(h_lev, 1)
                    n = SEQ // (2 * h)
                    link(V.tensor_tensor(sf[0], sf[0], pf[1][:, :, h - 1:h].to_broadcast([P, n, h]), ALU.mult))
                    link(V.tensor_tensor(pf[1], pf[1], pf[0][:, :, h - 1:h].to_broadcast([P, n, h]), ALU.mult))

                def mask(lv):
                    for hd in range(2):
                        dve.wait_ge(h_mm, 2 * (NPASS * t + lv) + hd + 1)
                        ps = PS[:, 4 + 2 * hd:6 + 2 * hd, :].rearrange("p u (c t) -> p (u c) t", t=P)
                        if lv == 0:
                            m = IDENT[:, :].unsqueeze(1).to_broadcast([P, BLK, P])
                            V.tensor_tensor(AT[:, hd], ps, m, ALU.mult).then_inc(h_at, 1)
                        else:
                            m = LEVELS[:, lv - 1, :].unsqueeze(1).to_broadcast([P, BLK, P])
                            dve.wait_ge(h_at, 2 * (NPASS * t + lv) + hd - 1)
                            V.copy_predicated(AT[:, hd], m, ps).then_inc(h_at, 1)
                if t:
                    dve.wait_ge(h_osq, t)
                level(1)
                if t < 3:
                    for i in range(LOOPED + EARLY * t, min(LOOPED + EARLY * t + EARLY, NBITS)):
                        one_bit(i, lambda ins, j: link(ins))
                mask(0)
                for lv in range(2, NPASS):
                    level(lv)
                    mask(lv - 1)
                dve.wait_ge(h_mm, 2 * NPASS * (t + 1) - 2)
                dve.wait_ge(h_lev, 7 * (t + 1))
                V.tensor_tensor(LV[:, 0], HK[:, 0:SEQ], SF, ALU.mult).then_inc(h_kt, 1)
                mask(NPASS - 1)
                dve.wait_ge(h_mm, 2 * NPASS * (t + 1))
                link(V.tensor_tensor(LV[:, 1], HQ[:, 0:SEQ], PF, ALU.mult))
                dve.wait_ge(h_u, t + 1)
                if t:
                    dve.wait_ge(sp_out, 16 * t)
                for c in range(BLK):
                    for hd in range(2):
                        rows = slice(64 * hd, 64 * hd + 64)
                        u = PS[rows, 6 + c // 4, P * (c % 4) + HD * hd:P * (c % 4) + HD * hd + HD]
                        last = V.scalar_tensor_tensor(SC[rows, c + 1, :], SC[rows, c, :], PF[rows, P * c + P - 1:P * c + P],
                                                      u, ALU.mult, ALU.add)
                        if hd == 0:
                            link(last)
                    last.then_inc(h_state, 1)
                    dve.wait_ge(h_state, BLK * t + c + 1)
                V.engine_nop().then_inc(hq_free, 1)
                dve.wait_ge(h_osq, t + 1)
                V.tensor_reduce(SS, OSQ.rearrange("p (c e) -> p c e", e=HD), AX.X, ALU.add).then_inc(h_ss, 1)
                dve.wait_ge(h_sd, t + 1)
                link(V.reciprocal(SR, SR))
                dve.wait_ge(rg_ready, 9)
                rg = RG[:, 0:BLK, P * t:P * t + P].rearrange("p c (u e) -> p u c e", e=HD)
                for hd in range(2):
                    r = SR.rearrange("p (u c) -> p u c", u=2)[:, hd].unsqueeze(2).to_broadcast([P, BLK, HD])
                    last = V.tensor_tensor(rg[:, hd], rg[:, hd], r, ALU.mult)
                link(last)
                for hd in range(2):
                    last = V.tensor_tensor(rg[:, hd], rg[:, hd], PS[:, 4 + hd, :].rearrange("p (c e) -> p c e", e=HD), ALU.mult)
                last.then_inc(h_orow, 1)

                if t == 2:
                    dve.wait_ge(h_orow, 3)
                    select()

            dve.wait_ge(h_orow, 4)

            def biggest(i):
                b, h = STEPS[i]
                n = P * (b + 1)
                dve.wait_ge(at_qk, i + 1)
                if i >= 2:
                    dve.wait_ge(at_tr, i - 1)
                bias = score(b) if b >= FIRST_TOPK else CAUSAL[:, P * (1 - b):2 * P]
                ps = PS[:, 4 + 2 * (i % 2):6 + 2 * (i % 2), :].rearrange("p u c -> p (u c)")[:, 0:n]
                link(V.tensor_tensor_reduce(SM[:, i % 2, 0:n], ps, bias, 1.0, NEG, ALU.add, ALU.max,
                                            accum_out=MX[:, i % 2:i % 2 + 1]))
                V.tensor_scalar(NMX[:, i % 2:i % 2 + 1], MX[:, i % 2:i % 2 + 1], -1.0, None, ALU.mult).then_inc(at_sm, 1)

            def normalise(bi):
                dve.wait_ge(at_pv, H * (bi + 1))
                dve.wait_ge(at_exp, H * (bi + 1))
                if bi >= 2:
                    dve.wait_ge(at_ott, bi - 1)
                link(V.reciprocal(RSUM, SUMS[:, bi % 2, :]))
                V.tensor_tensor(OTOK[:, bi % 2, :].rearrange("p (h d) -> p h d", d=HD),
                                PS[:, 2, :].rearrange("p (h d) -> p h d", d=HD),
                                RSUM.unsqueeze(2).to_broadcast([P, H, HD]), ALU.mult).then_inc(at_on, 1)
            for i in range(64):
                biggest(i)
                if i and i % H == 0:
                    normalise(i // H - 1)
            normalise(7)

            dve.wait_ge(at_tr, 64)
            for g in range(GRP):
                rows = slice(64 * g, 64 * g + 64)
                V.tensor_copy(KTD[rows, :, TOPK:TOPK + 1], K3[rows, g, SEQ:TOK].unsqueeze(2)).then_inc(d_ktc, 1)
            dve.wait_ge(s0_in, 64)
            dve.wait_ge(vb_in, 16 * 8)
            for t in range(4):
                f, k, q = (HD3[:, w, t, :].unsqueeze(2).to_broadcast([P, NB, HD]) for w in range(3))
                V.tensor_tensor(T1[:, t], S0[:, t], f, ALU.mult)
                link(V.tensor_tensor(T2[:, t], VB[:, t], k, ALU.mult))
                last = V.tensor_tensor(T1[:, t], T1[:, t], T2[:, t], ALU.add)
                if t < 3:
                    link(last)
            last.then_inc(ds_new, 1)
            dve.wait_ge(ds_new, 1)
            for t in range(4):
                q = HD3[:, 2, t, :].unsqueeze(2).to_broadcast([P, NB, HD])
                last = V.tensor_tensor(T2[:, t], T1[:, t], q, ALU.mult)
            last.then_inc(ds_prod, 1)
            dve.wait_ge(d_qk, 1)
            link(V.tensor_copy(SDD, PS[0:H, 0:NB, 0:TOPK + 1]))
            link(V.tensor_scalar(NFW, NF, -MASKED, None, ALU.mult))
            link(V.tensor_tensor(SDD[:, :, TOPK - 1], SDD[:, :, TOPK - 1], NFW, ALU.add))
            link(V.tensor_scalar(NFW, NF, 1.0, MASKED, ALU.subtract, ALU.mult))
            link(V.tensor_tensor(SDD[:, :, TOPK], SDD[:, :, TOPK], NFW, ALU.add))
            link(V.tensor_reduce(DMX, SDD, AX.X, ALU.max))
            V.tensor_tensor(SDD, SDD, DMX.unsqueeze(2).to_broadcast([H, NB, TOPK + 1]), ALU.subtract).then_inc(d_sub, 1)
            dve.wait_ge(d_exp, 1)
            link(V.tensor_reduce(DSUM, SDD, AX.X, ALU.add))
            link(V.reciprocal(DSUM, DSUM))
            V.tensor_tensor(SDD, SDD, DSUM.unsqueeze(2).to_broadcast([H, NB, TOPK + 1]), ALU.mult).then_inc(d_p, 1)
            dve.wait_ge(d_pt, 1)
            V.tensor_copy(PTD.rearrange("p j h -> p (j h)"), PS[:, 4, 0:P]).then_inc(d_ptc, 1)
            V.tensor_copy(PTN.rearrange("p b h -> p (b h)"), PS[0:1, 5, 0:64]).then_inc(d_ptc, 1)
            dve.wait_ge(or_in, 16)
            orow = OD8[:, 512:1024].rearrange("p (h e) -> p h e", e=HD)
            osq = OD8SQ.rearrange("p (h e) -> p h e", e=HD)
            link(V.tensor_tensor(osq, orow, orow, ALU.mult))
            V.tensor_reduce(DSS, osq, AX.X, ALU.add).then_inc(ds_ss, 1)
            dve.wait_ge(ds_sd, 1)
            link(V.reciprocal(DSS, DSS))
            link(V.tensor_tensor(orow, orow, DSS.unsqueeze(2).to_broadcast([NB, H, HD]), ALU.mult))
            dve.wait_ge(oa_in, 16)
            V.tensor_tensor(OD8[:, 512:1024], OD8[:, 512:1024], RG[0:NB, 8, :], ALU.mult).then_inc(od8_ready, 1)
            dve.wait_ge(od8_mm, 1)
            ot = PS[:, 4, 0:64].rearrange("p (k b) -> p k b", b=NB)
            V.tensor_copy(OTA[:, :, SEQ:TOK], ot[:, 0:4, :]).then_inc(ot_ready, 1)
            V.tensor_copy(OTR[:, :, SEQ:TOK], ot[:, 4:8, :]).then_inc(ot_ready, 1)
            for d in range(DT):
                for tg in range(TG):
                    residual(1, d, tg, d % 2, ALPHA)
            norm(1)

        block = ctx.enter_context(nc.Block())

        @block.sync
        def _(sp):
            sp.dma_start(XIN[:, 0:BLK, :], I["x_prompt"][0].rearrange("(b p) d -> p b d", p=P)).then_inc(x_loaded, 16)
            sp.dma_start(XIN[0:NB, BLK, :], I["x_sample"][:, 0, :]).then_inc(x_loaded, 16)

            def ring(n, parts):
                if 4 <= n < MIX0 + 4:
                    sp.wait_ge(up_done, 6 * ((n - 4) // 2 + 1))
                elif n >= MIX0 + 4:
                    m = n - 4 - MIX0
                    if m < 14:
                        sp.wait_ge(unit_done, max(u for u in range(len(UNITS)) if UNITS[u][2] == m) + 1)
                    else:
                        sp.wait_ge(y_done, 24 + 6 * (m - 13))
                at = 0
                for w, c0, width in parts:
                    whole = sum(x[2] for x in parts)
                    dst = RING[:, n % 4, 0:DT * whole].rearrange("p (k c) -> p k c", c=whole)
                    sp.dma_start(dst[:, :, at:at + width], w[:, :, c0:c0 + width]).then_inc(ring_in[n % 4], 16)
                    at += width

            def ffn_loads(ff, names):
                wg, wu = (I[x][0].rearrange("(k p) n -> p k n", p=P) for x in names[:2])
                wd = I[names[2]][0].rearrange("(f p) n -> p f n", p=P)
                n0 = ITEM0[ff]
                for s in (0, 1):
                    ring(n0 + 2 * s, [(wg, SLAB * s, SLAB)])
                    ring(n0 + 2 * s + 1, [(wu, SLAB * s, SLAB)])
                for slot in range(2):
                    if ff:
                        sp.wait_ge(y_done, 48)
                        sp.wait_ge(ss_out, 64)
                    sp.dma_start(WD[:, slot, :].rearrange("p (f c) -> p f c", c=P),
                                 wd[:, :, P * slot:P * slot + P]).then_inc(wd_in[slot], 16)

                def slab(s, odd):
                    for u, w in enumerate((wg, wu)):
                        if u == 0:
                            sp.wait_ge(up_done, 6 * s + (66 * ff - 6))
                        sp.dma_start(RING[:, 2 * odd + u, :].rearrange("p (k c) -> p k c", c=SLAB),
                                     w[:, :, bass.ds(s * SLAB, SLAB)]).then_inc(ring_in[2 * odd + u], 16)
                with sp.Fori(1, NSLAB // 2) as i:
                    slab(2 * i, 0)
                    slab(2 * i + 1, 1)
                slab(NSLAB - 1, 0)
                with sp.Fori(1, DT // 2) as i:
                    d = 2 * i
                    for slot in range(2):
                        sp.wait_ge(y_done, 3 * d + (48 * ff + 3 * slot - 3))
                        sp.dma_start(WD[:, slot, :].rearrange("p (f c) -> p f c", c=P),
                                     wd[:, :, bass.ds(d * P + P * slot, P)]).then_inc(wd_in[slot], 16)

            ffn_loads(0, ("ffn1_wg", "ffn1_wu", "ffn1_wd"))
            for m, parts in enumerate(MIX):
                ring(MIX0 + m, parts)
            ffn_loads(1, ("ffn2_wg", "ffn2_wu", "ffn2_wd"))

        @block.tensor
        def _(pe):
            def turn_in():
                pe.wait_ge(consts, 1)
                pe.wait_ge(x_loaded, 32)
                for b in range(9):
                    rows = P if b < BLK else NB
                    for half in range(2):
                        u = 2 * b + half
                        if u >= 8:
                            pe.wait_ge(x_ready, u - 7)
                        for k in range(4):
                            last = nc.tensor.transpose(PS[:, u % 8, k * P:k * P + rows],
                                                       XIN[0:rows, b, (4 * half + k) * P:(4 * half + k + 1) * P],
                                                       IDENT[0:rows, 0:rows])
                        last.then_inc(x_turned, 1)

            def cols(tg):
                return slice(TW * tg, TW * tg + TW)

            def up_slab(ff, s, odd, first):
                for j in range(2):
                    for tg in range(TG):
                        for u in range(2):
                            if j == 0 and tg == 0:
                                base = reach[ITEM0[ff] + 2 * odd + u]
                                pe.wait_ge(ring_in[2 * odd + u], 8 * (s - odd) + base)
                            if not (first and j == 0) and u == 0:
                                pe.wait_ge(h_done, 66 * ff + 6 * s + (3 * j - 3 + tg + 1))
                            w = RING[:, 2 * odd + u, :].rearrange("p (k c) -> p k c", c=SLAB)
                            for k in range(DT):
                                last = nc.tensor.matmul(PS[:, 3 * u + tg, 0:TW], w[:, k, j * P:j * P + P],
                                                        ACTS[:, k, cols(tg)], start=k == 0, stop=k == DT - 1)
                            if u == 1:
                                last.then_inc(up_done, 1)

            def ffn(ff):
                ln = 2 * ff
                up_slab(ff, 0, 0, True)
                with pe.Fori(0, NSLAB // 2) as i:
                    up_slab(ff, 2 * i + 1, 1, False)
                    up_slab(ff, 2 * i + 2, 0, False)
                pe.wait_ge(h_done, 66 * ff + 3 * FT)

                def down(d, slot, first):
                    pe.wait_ge(wd_in[slot], 8 * (d - slot) + (16 * (4 * ff + 1)))
                    w = WD[:, slot, :].rearrange("p (f c) -> p f c", c=P)
                    for tg in range(TG):
                        if not first:
                            pe.wait_ge(z_done, 24 * ln + 3 * d + (tg + 1 - 6))
                        for f in range(FT):
                            last = nc.tensor.matmul(PS[:, 3 * slot + tg, 0:TW], w[:, f, :], HT[:, f, cols(tg)],
                                                    start=f == 0, stop=f == FT - 1)
                        last.then_inc(y_done, 1)
                down(0, 0, True)
                down(1, 1, True)
                with pe.Fori(1, DT // 2) as i:
                    down(2 * i, 0, False)
                    down(2 * i + 1, 1, False)
                norm_stats(ln)

            def norm_stats(n):
                def mean(tg):
                    pe.wait_ge(ln_sum, 24 * n + DT * TG - TG + tg + 1)
                    nc.tensor.matmul(PS[:, tg, 0:TW], MEAN1[:, :], SUM[:, tg, :], start=True, stop=True)\
                        .then_inc(ln_mean, 1)

                def var(tg):
                    pe.wait_ge(ln_vs, 3 * n + tg + 1)
                    nc.tensor.matmul(PS[:, 3 + tg, 0:TW], MEAN1[:, :], VAR[:, tg, :], start=True, stop=True)\
                        .then_inc(ln_var, 1)
                for tg in range(TG):
                    mean(tg)
                for tg in range(TG):
                    var(tg)

            def turn_out():
                for b in range(9):
                    rows = P if b < BLK else NB
                    for half in range(2):
                        u = 2 * b + half
                        if u >= 8:
                            pe.wait_ge(y_copied, u - 7)
                        for k in range(4):
                            last = nc.tensor.transpose(PS[0:rows, u % 8, k * P:k * P + P],
                                                       ACTS[:, 4 * half + k, b * P:b * P + rows], IDENT[:, :])
                        last.then_inc(y_turned, 1)

            turn_in()
            pe.wait_ge(x_ready, 18)
            pe.wait_ge(consts2, 1)
            ffn(0)
            pe.wait_ge(ln_done, 0 + TG)
            if MIXER:
                pe_mixer(pe, cols, norm_stats)
                pe.wait_ge(ln_done, 3 + TG)
            ffn(1)
            pe.wait_ge(ln_done, 6 + TG)
            turn_out()

        @block.scalar
        def _(act):
            A = nc.scalar.activation
            step = [0]

            def link(ins):
                step[0] += 1
                ins.then_inc(act_step, 1)
                act.wait_ge(act_step, step[0])

            act.wait_ge(consts, 1)
            A(SMALL[:, 236:237], IDENT[:, 0:1], ACT.Silu)

            def ffn(ff):
                def silu(s, j, tg, first):
                    act.wait_ge(up_done, 66 * ff + 6 * s + (3 * j + tg + 1))
                    if not first:
                        act.wait_ge(h_done, 66 * ff + 6 * s + (3 * j + tg + 1 - 3))
                    A(SG[:, tg, :], PS[:, tg, 0:TW], ACT.Silu).then_inc(silu_done, 1)
                for j in range(2):
                    for tg in range(TG):
                        silu(0, j, tg, j == 0)
                with act.Fori(1, NSLAB) as s:
                    for j in range(2):
                        for tg in range(TG):
                            silu(s, j, tg, False)

            def norm(n):
                def square(tg):
                    act.wait_ge(ln_xc, 3 * n + tg + 1)
                    if tg == 2:
                        act.wait_ge(ln_vs, 3 * n + 1)
                    A(SQ[:, tg % 2], ACTS[:, :, TW * tg:TW * tg + TW], ACT.Square).then_inc(ln_sq, 1)

                def sd(tg):
                    act.wait_ge(ln_var, 3 * n + tg + 1)
                    A(RSTD[:, tg, :], PS[:, 3 + tg, 0:TW], ACT.Sqrt, bias=EPS[:, (0, 1, 0)[n]:(0, 1, 0)[n] + 1])\
                        .then_inc(ln_sd, 1)

                def gain(tg):
                    act.wait_ge(ln_n, 3 * n + tg + 1)
                    for d in range(DT):
                        a = ACTS[:, d, TW * tg:TW * tg + TW]
                        last = A(a, a, ACT.Identity, scale=PARAMS[:, 2 * n, d:d + 1], bias=PARAMS[:, 2 * n + 1, d:d + 1])
                    last.then_inc(ln_done, 1)
                act.wait_ge(params_in, 96)
                square(0)
                square(1)
                sd(0)
                square(2)
                gain(0)
                sd(1)
                gain(1)
                sd(2)
                gain(2)

            act.wait_ge(consts2, 1)
            ffn(0)
            norm(0)
            if MIXER:
                act_mixer(act, A, link)
                norm(1)
            A(SMALL[:, 237:238], IDENT[:, 0:1], ACT.Silu)
            ffn(1)
            norm(2)
            for b in range(9):
                rows = P if b < BLK else NB
                act.wait_ge(y_turned, 2 * b + 2)
                if b >= 2:
                    act.wait_ge(y_stored[b % 2], 16 * (b // 2))
                dst = XOUT[0:rows, b % 2, :].rearrange("p (u d) -> p u d", d=512)
                A(dst, PS[0:rows, 2 * b % 8:2 * b % 8 + 2, :], ACT.Copy).then_inc(y_copied, 2)

        @block.vector
        def _(dve):
            V = nc.vector
            step = [0]

            def link(ins):
                step[0] += 1
                ins.then_inc(dve_step, 1)
                dve.wait_ge(dve_step, step[0])

            for u in range(18):
                b, half = divmod(u, 2)
                rows = P if b < BLK else NB
                dve.wait_ge(x_turned, u + 1)
                V.tensor_copy(ACTS[:, 4 * half:4 * half + 4, b * P:b * P + rows],
                              PS[:, u % 8, :].rearrange("p (k t) -> p k t", t=P)[:, :, 0:rows]).then_inc(x_ready, 1)
            dve.wait_ge(x_ready, 18)

            def residual(n, d, tg, slot, factor):
                dve.wait_ge(y_done, 24 * n + 3 * d + (tg + 1))
                a = ACTS[:, bass.ds(d, 1), TW * tg:TW * tg + TW].rearrange("p o t -> p (o t)")
                V.scalar_tensor_tensor(a, a, factor, PS[:, 3 * slot + tg, 0:TW], ALU.mult, ALU.add)\
                    .then_inc(z_done, 1)

            def ffn(ff):
                def hidden(s, j, tg):
                    dve.wait_ge(silu_done, 66 * ff + 6 * s + (3 * j + tg + 1))
                    out = HT[:, bass.ds(2 * s + j, 1), TW * tg:TW * tg + TW].rearrange("p o t -> p (o t)")
                    V.tensor_tensor(out, SG[:, tg, :], PS[:, 3 + tg, 0:TW], ALU.mult).then_inc(h_done, 1)
                with dve.Fori(0, NSLAB) as s:
                    for j in range(2):
                        for tg in range(TG):
                            hidden(s, j, tg)
                with dve.Fori(0, DT // 2) as i:
                    d = 2 * i
                    for slot in range(2):
                        for tg in range(TG):
                            residual(2 * ff, d + slot, tg, slot, 2 * ALPHA)
                norm(2 * ff)

            def norm(n):
                def group(tg):
                    return ACTS[:, :, TW * tg:TW * tg + TW]

                def centre(tg):
                    dve.wait_ge(ln_mean, 3 * n + tg + 1)
                    dve.wait_ge(ln_sum, 24 * n + DT * TG)
                    V.tensor_tensor(group(tg), group(tg), PS[:, tg:tg + 1, 0:TW].to_broadcast([P, DT, TW]),
                                    ALU.subtract).then_inc(ln_xc, 1)

                def sqsum(tg):
                    dve.wait_ge(ln_sq, 3 * n + tg + 1)
                    V.tensor_reduce(VAR[:, tg, :], SQ[:, tg % 2].rearrange("p d t -> p t d"), AX.X, ALU.add)\
                        .then_inc(ln_vs, 1)

                def scale(tg):
                    dve.wait_ge(ln_sd, 3 * n + tg + 1)
                    link(V.reciprocal(RSTD[:, tg, :], RSTD[:, tg, :]))
                    V.tensor_tensor(group(tg), group(tg), RSTD[:, tg:tg + 1, :].to_broadcast([P, DT, TW]),
                                    ALU.mult).then_inc(ln_n, 1)
                centre(0)
                centre(1)
                sqsum(0)
                centre(2)
                sqsum(1)
                scale(0)
                sqsum(2)
                scale(1)
                scale(2)

            if MIXER:
                dve_consts(dve, V, link)
            dve.wait_ge(consts2, 1)
            ffn(0)
            if MIXER:
                dve_mixer(dve, V, link, step, residual, norm)
            ffn(1)

        @block.gpsimd
        def _(pool):
            G = nc.gpsimd
            step = [0]

            def link(ins):
                step[0] += 1
                ins.then_inc(pool_step, 1)
                pool.wait_ge(pool_step, step[0])

            link(G.memset(IDENT[:, :], 0.0))
            G.affine_select(out=IDENT[:, :], in_=IDENT[:, :], compare_op=ALU.not_equal, fill=1.0, base=0,
                            pattern=[[-1, P]], channel_multiplier=1).then_inc(consts, 1)
            G.memset(MEAN1[:, :], 1.0 / D)
            G.memset(EPS[:, 0:1], 4 * LN_EPS)
            G.memset(EPS[:, 1:2], LN_EPS)
            G.memset(EPS[:, 2:3], RMS_EPS).then_inc(consts2, 1)
            with nc.allow_non_contiguous_dma(reason="gains and biases, feature-major"):
                for i, name in enumerate(("ln1_g", "ln1_b", "ln2_g", "ln2_b", "ln3_g", "ln3_b")):
                    pool.dma_start(PARAMS[:, i, :], I[name][0].rearrange("(k p) -> p k", p=P)).then_inc(params_in, 16)
            if MIXER:
                pool_consts(pool, G, link)

            def sums(n):
                for d in range(DT):
                    for tg in range(TG):
                        pool.wait_ge(z_done, 24 * n + 3 * d + tg + 1)
                        a = ACTS[:, d, TW * tg:TW * tg + TW]
                        if d == 0:
                            G.tensor_copy(SUM[:, tg, :], a).then_inc(ln_sum, 1)
                        else:
                            pool.wait_ge(ln_sum, 24 * n + 3 * d - 3 + tg + 1)
                            G.tensor_tensor(SUM[:, tg, :], SUM[:, tg, :], a, ALU.add).then_inc(ln_sum, 1)
            sums(0)
            if MIXER:
                pool_mixer(pool, G, link)
                sums(1)
            sums(2)
            for b in range(9):
                pool.wait_ge(y_copied, 2 * b + 2)
                if b < BLK:
                    pool.dma_start(O["y_prompt"][0, b * P:b * P + P, :], XOUT[:, b % 2, :]).then_inc(y_stored[b % 2], 16)
                else:
                    pool.dma_start(O["y_sample"][:, 0, :], XOUT[0:NB, b % 2, :]).then_inc(y_stored[b % 2], 16)
            pool.wait_ge(y_stored[0], 16 * 5)
            pool.wait_ge(y_stored[1], 16 * 4)


_INS = ["x_prompt", "x_sample", "cache_k", "cache_v", "cache_kidx", "state_hgrn", "page_table", "w_in", "w_out",
        "hgrn_lb", "hgrn_norm_g", "ffn1_wg", "ffn1_wu", "ffn1_wd", "ffn2_wg", "ffn2_wu", "ffn2_wd",
        "ln1_g", "ln1_b", "ln2_g", "ln2_b", "ln3_g", "ln3_b"]
_OUTS = [("y_prompt", (1, 1024, 1024)), ("y_sample", (8, 1, 1024)), ("k_prompt", (1, 1, 1024, 2, 64)),
         ("v_prompt", (1, 1, 1024, 2, 64)), ("kidx_prompt", (1, 1, 1024, 64)), ("state_prompt", (1, 1, 8, 64, 64)),
         ("k_sample", (1, 8, 1, 2, 64)), ("v_sample", (1, 8, 1, 2, 64)), ("kidx_sample", (1, 8, 1, 64)),
         ("state_sample", (1, 8, 8, 64, 64))]


def kernel(**inputs):
    import concourse.bacc as bacc
    from concourse.bass_utils import run_bass_kernel_spmd

    nc = bacc.Bacc("TRN2", target_bir_lowering=False, num_devices=1)
    arrays, ins, outs = {}, {}, {}
    for name in _INS:
        a = np.ascontiguousarray(inputs[name])
        arrays[name] = a
        ins[name] = nc.dram_tensor(name, a.shape, mybir.dt.from_np(a.dtype), kind="ExternalInput").ap()
    for name, shape in _OUTS:
        outs[name] = nc.dram_tensor("out_" + name, shape, mybir.dt.float32, kind="ExternalOutput").ap()
    build_decoder_step(nc, ins, outs)
    r = run_bass_kernel_spmd(nc, [arrays], core_ids=[0])
    return tuple(r.results[0]["out_" + name] for name, _ in _OUTS)
```
